# Optimizing a Trainium2 kernel written in Bass

```python
import math, functools
import jax, jax.numpy as jnp
from jax import lax
import numpy as np

D_MODEL = 1024
BATCH = 1
SEQ = 1024
DEPTH = 2

GRID_W = 64
CTX_LEN = 256
HEAD_DIM = 64
ROPE_THETA = 10000.0
NORM_EPS = 1e-6
Q_BLOCK = 128
MIX_WIDTH = D_MODEL

A_HEADS = (MIX_WIDTH // 2) // (2 * HEAD_DIM)
A_QK = A_HEADS * 2 * HEAD_DIM
A_VDIM = 2 * HEAD_DIM
A_WIDTH = A_HEADS * A_VDIM
B_HEADS = (MIX_WIDTH // 2) // HEAD_DIM
B_WIDTH = B_HEADS * HEAD_DIM
NA_ROWS = 8
NA_COLS = 16
EVEN_IN = 2 * A_QK + A_WIDTH + 3 * B_WIDTH

C_HEADS = (MIX_WIDTH // 2) // HEAD_DIM
C_KV_HEADS = 2
C_REP = C_HEADS // C_KV_HEADS
C_Q = C_HEADS * HEAD_DIM
C_KV = C_KV_HEADS * HEAD_DIM
WINDOW = 128
D_HEADDIM = 64
D_INNER = MIX_WIDTH // 2
D_HEADS = D_INNER // D_HEADDIM
D_GROUPS = 2
D_HPG = D_HEADS // D_GROUPS
D_STATE = 128
D_CONV = 5
D_XBC = D_INNER + 2 * D_GROUPS * D_STATE
SSD_CHUNK = 128
ODD_IN = C_Q + 2 * C_KV + D_XBC + D_INNER + 2 * D_HEADS

N_EXPERTS = 16
EXPERT_FF = D_MODEL
CAPACITY_FACTOR = 2

kernel_name = 'hybrid_diffusion_trunk_diffattn_natten_swa_ssd_ecmoe'

def rmsnorm(u, g):
    uf = u.astype(jnp.float32)
    y = uf * lax.rsqrt(jnp.mean(uf * uf, axis=-1, keepdims=True) + NORM_EPS)
    return (y * g.astype(jnp.float32)).astype(u.dtype)

def split_cols(p, sizes):
    return jnp.split(p, np.cumsum(sizes)[:-1].tolist(), axis=-1)

def ada_modulation(cond, w_mod, b_mod):
    mod = jax.nn.silu(cond) @ w_mod + b_mod
    return jnp.split(mod[..., None, :], 6, axis=-1)

def axial_rope_tables(n):
    t = jnp.arange(n, dtype=jnp.int32)
    row = (t // GRID_W).astype(jnp.float32)
    col = (t % GRID_W).astype(jnp.float32)
    n_freq = HEAD_DIM // 4
    inv_freq = ROPE_THETA ** (-jnp.arange(n_freq, dtype=jnp.float32) / n_freq)
    ang = jnp.concatenate([row[:, None] * inv_freq, col[:, None] * inv_freq], axis=-1)
    return jnp.cos(ang), jnp.sin(ang)

def apply_rope(u, cos, sin):
    uf = u.astype(jnp.float32).reshape(u.shape[:-1] + (HEAD_DIM // 2, 2))
    u1, u2 = uf[..., 0], uf[..., 1]
    cs, sn = cos[:, None, :], sin[:, None, :]
    out = jnp.stack([u1 * cs - u2 * sn, u1 * sn + u2 * cs], axis=-1)
    return out.reshape(u.shape).astype(u.dtype)

def differential_attention(q, k, v, lam):
    scale = q.shape[-1] ** -0.5
    s = jnp.einsum('bqhmd,bkhmd->bhmqk', q, k).astype(jnp.float32) * scale
    p = jax.nn.softmax(s, axis=-1)
    a = (p[:, :, 0] - lam * p[:, :, 1]).astype(v.dtype)
    return jnp.einsum('bhqk,bkhe->bqhe', a, v)

def context_attention(q, k, v):
    b, m, _, d = q.shape
    s = jnp.einsum('bqhd,bkhd->bhqk', q, k).astype(jnp.float32) * d ** -0.5
    p = jax.nn.softmax(s, axis=-1).astype(v.dtype)
    return jnp.einsum('bhqk,bkhd->bqhd', p, v).reshape(b, m, -1)

def neighbourhood_attention(q, k, v, k_ctx, v_ctx, rpb):
    b, n, nh, d = q.shape
    rows = n // GRID_W
    kh, kw = min(NA_ROWS, rows), NA_COLS
    qg = q.reshape(b, rows, GRID_W, nh, d)
    kg = k.reshape(b, rows, GRID_W, nh, d)
    vg = v.reshape(b, rows, GRID_W, nh, d)
    r_idx = jnp.arange(rows)
    row_start = jnp.clip(r_idx - kh // 2, 0, rows - kh)
    w_idx = jnp.arange(GRID_W)
    col_idx = jnp.clip(w_idx - kw // 2, 0, GRID_W - kw)[:, None] + jnp.arange(kw)
    rel_c = col_idx - w_idx[:, None] + NA_COLS - 1
    scale = d ** -0.5
    n_keys = kh * kw

    def row_block(args):
        q_r, r, rs = args
        k_rows = lax.dynamic_slice_in_dim(kg, rs, kh, axis=1)
        v_rows = lax.dynamic_slice_in_dim(vg, rs, kh, axis=1)
        k_nb = k_rows[:, :, col_idx].transpose(0, 2, 1, 3, 4, 5).reshape(b, GRID_W, n_keys, nh, d)
        v_nb = v_rows[:, :, col_idx].transpose(0, 2, 1, 3, 4, 5).reshape(b, GRID_W, n_keys, nh, d)
        rel_r = rs + jnp.arange(kh) - r + NA_ROWS - 1
        bias = rpb[:, rel_r[None, :, None], rel_c[:, None, :]].reshape(nh, GRID_W, n_keys)
        s_nb = jnp.einsum('bwhd,bwkhd->bhwk', q_r, k_nb).astype(jnp.float32) * scale + bias.astype(jnp.float32)
        s_cx = jnp.einsum('bwhd,bmhd->bhwm', q_r, k_ctx).astype(jnp.float32) * scale
        p = jax.nn.softmax(jnp.concatenate([s_nb, s_cx], axis=-1), axis=-1).astype(v.dtype)
        return (jnp.einsum('bhwk,bwkhd->bwhd', p[..., :n_keys], v_nb)
                + jnp.einsum('bhwm,bmhd->bwhd', p[..., n_keys:], v_ctx))

    o = lax.map(row_block, (qg.transpose(1, 0, 2, 3, 4), r_idx, row_start))
    return o.transpose(1, 0, 2, 3, 4).reshape(b, n, nh * d)

def window_attention_with_sink(q, k, v, k_ctx, v_ctx, sinks):
    b, n, g, r, d = q.shape
    m = k_ctx.shape[1]
    nb = n // Q_BLOCK
    side = -(-WINDOW // Q_BLOCK)
    span = (2 * side + 1) * Q_BLOCK
    pad = ((0, 0), (side * Q_BLOCK, side * Q_BLOCK), (0, 0), (0, 0))
    kp = jnp.pad(k, pad)
    vp = jnp.pad(v, pad)
    sink = jnp.broadcast_to(sinks.astype(jnp.float32).reshape(1, g, r, 1, 1), (b, g, r, Q_BLOCK, 1))
    scale = d ** -0.5
    q_blocks = q.reshape(b, nb, Q_BLOCK, g, r, d).swapaxes(0, 1)

    def block(args):
        qb, blk = args
        kb = lax.dynamic_slice_in_dim(kp, blk * Q_BLOCK, span, axis=1)
        vb = lax.dynamic_slice_in_dim(vp, blk * Q_BLOCK, span, axis=1)
        qpos = blk * Q_BLOCK + jnp.arange(Q_BLOCK)
        kpos = (blk - side) * Q_BLOCK + jnp.arange(span)
        valid = (jnp.abs(qpos[:, None] - kpos[None, :]) <= WINDOW) & (kpos >= 0) & (kpos < n)
        s_loc = jnp.einsum('bqgrd,bkgd->bgrqk', qb, kb).astype(jnp.float32) * scale
        s_loc = jnp.where(valid, s_loc, -jnp.inf)
        s_ctx = jnp.einsum('bqgrd,bmgd->bgrqm', qb, k_ctx).astype(jnp.float32) * scale
        p = jax.nn.softmax(jnp.concatenate([s_loc, s_ctx, sink], axis=-1), axis=-1).astype(v.dtype)
        return (jnp.einsum('bgrqk,bkgd->bqgrd', p[..., :span], vb)
                + jnp.einsum('bgrqm,bmgd->bqgrd', p[..., span:span + m], v_ctx))

    o = lax.map(block, (q_blocks, jnp.arange(nb)))
    return o.swapaxes(0, 1).reshape(b, n, g * r * d)

def sink_attention(q, k, v, sinks):
    b, m, g, r, d = q.shape
    s = jnp.einsum('bqgrd,bkgd->bgrqk', q, k).astype(jnp.float32) * d ** -0.5
    sk = jnp.broadcast_to(sinks.astype(jnp.float32).reshape(1, g, r, 1, 1), (b, g, r, m, 1))
    p = jax.nn.softmax(jnp.concatenate([s, sk], axis=-1), axis=-1)[..., :m].astype(v.dtype)
    return jnp.einsum('bgrqk,bkgd->bqgrd', p, v).reshape(b, m, g * r * d)

def depthwise_conv_silu(u, w, bias):
    y = lax.conv_general_dilated(u, w.astype(u.dtype), window_strides=(1,),
                                 padding=((D_CONV // 2, D_CONV // 2),),
                                 dimension_numbers=('NWC', 'WIO', 'NWC'),
                                 feature_group_count=u.shape[-1])
    return jax.nn.silu(y + bias)

def ssd_prep(xbc, dt_raw, conv_w, conv_b, dt_bias_f, dt_bias_b):
    b, L, _ = xbc.shape
    u = depthwise_conv_silu(xbc, conv_w, conv_b).astype(jnp.float32)
    xs, bm, cm = split_cols(u, (D_INNER, D_GROUPS * D_STATE, D_GROUPS * D_STATE))
    xs = xs.reshape(b, L, D_GROUPS, D_HPG, D_HEADDIM)
    bm = bm.reshape(b, L, D_GROUPS, D_STATE)
    cm = cm.reshape(b, L, D_GROUPS, D_STATE)
    dt_raw = dt_raw.astype(jnp.float32)
    dtf = jax.nn.softplus(dt_raw[..., :D_HEADS] + dt_bias_f.astype(jnp.float32)).reshape(b, L, D_GROUPS, D_HPG)
    dtb = jax.nn.softplus(dt_raw[..., D_HEADS:] + dt_bias_b.astype(jnp.float32)).reshape(b, L, D_GROUPS, D_HPG)
    return xs, bm, cm, dtf, dtb

def ssd_chunked(x, dt, a, bm, cm, init_state, want_y):
    b, L, g, r, p = x.shape
    nst = bm.shape[-1]
    nc = L // SSD_CHUNK
    x = x.reshape(b, nc, SSD_CHUNK, g, r, p)
    dt = dt.reshape(b, nc, SSD_CHUNK, g, r)
    bm = bm.reshape(b, nc, SSD_CHUNK, g, nst)
    cm = cm.reshape(b, nc, SSD_CHUNK, g, nst)
    cum = jnp.cumsum(dt * a, axis=2)
    last = cum[:, :, -1]
    xdt = x * dt[..., None]
    states = jnp.einsum('bcsgn,bcsgrp->bcgrpn', bm, xdt * jnp.exp(last[:, :, None] - cum)[..., None])

    def step(carry, inp):
        st, dec = inp
        return carry * dec[..., None, None] + st, carry

    final, prev = lax.scan(step, init_state, (states.swapaxes(0, 1), jnp.exp(last).swapaxes(0, 1)))
    if not want_y:
        return None, final
    prev = prev.swapaxes(0, 1)
    diff = cum[:, :, :, None] - cum[:, :, None, :]
    causal = jnp.tril(jnp.ones((SSD_CHUNK, SSD_CHUNK), dtype=bool))[:, :, None, None]
    lmat = jnp.exp(jnp.where(causal, diff, -jnp.inf))
    cb = jnp.einsum('bclgn,bcsgn->bclsg', cm, bm)
    y_diag = jnp.einsum('bclsgr,bcsgrp->bclgrp', cb[..., None] * lmat, xdt)
    y_off = jnp.einsum('bclgn,bcgrpn->bclgrp', cm, prev) * jnp.exp(cum)[..., None]
    return (y_diag + y_off).reshape(b, L, g, r, p), final

def ssd_output(y, xs, z, d_skip, gnorm_g):
    b, L = y.shape[:2]
    y = y + d_skip.astype(jnp.float32).reshape(D_GROUPS, D_HPG)[:, :, None] * xs
    y = y.reshape(b, L, D_INNER) * jax.nn.silu(z.astype(jnp.float32))
    y = y.reshape(b, L, D_GROUPS, D_INNER // D_GROUPS)
    y = y * lax.rsqrt(jnp.mean(y * y, axis=-1, keepdims=True) + NORM_EPS)
    return y.reshape(b, L, D_INNER) * gnorm_g.astype(jnp.float32)

def expert_choice_ffn(h, w_router, w_gate, w_up, w_down):
    b, n, _ = h.shape
    cap = CAPACITY_FACTOR * n // N_EXPERTS
    aff = jax.nn.softmax(jnp.einsum('bnd,de->bne', h, w_router).astype(jnp.float32), axis=-1)
    gate, idx = lax.top_k(jnp.swapaxes(aff, 1, 2), cap)
    bidx = jnp.arange(b)[:, None, None]
    xg = h[bidx, idx]
    hid = jax.nn.silu(jnp.einsum('becd,edf->becf', xg, w_gate)) * jnp.einsum('becd,edf->becf', xg, w_up)
    out = jnp.einsum('becf,efd->becd', hid, w_down) * gate[..., None].astype(h.dtype)
    return jnp.zeros_like(h).at[bidx, idx].add(out)

def mixer_even(h, hc, ctx_out, *, layer_idx, w_in, w_out, lam_q1, lam_k1, lam_q2, lam_k2, subln_g, rpb):
    b, n, _ = h.shape
    m = hc.shape[1]
    sizes = (A_QK, A_QK, A_WIDTH, B_WIDTH, B_WIDTH, B_WIDTH)
    qa, ka, va, qb, kb, vb = split_cols(h @ w_in, sizes)
    qa_c, ka_c, va_c, qb_c, kb_c, vb_c = split_cols(hc @ w_in, sizes)
    cos, sin = axial_rope_tables(n)
    qa = apply_rope(qa.reshape(b, n, 2 * A_HEADS, HEAD_DIM), cos, sin).reshape(b, n, A_HEADS, 2, HEAD_DIM)
    ka = apply_rope(ka.reshape(b, n, 2 * A_HEADS, HEAD_DIM), cos, sin).reshape(b, n, A_HEADS, 2, HEAD_DIM)
    va = va.reshape(b, n, A_HEADS, A_VDIM)
    ka_c = ka_c.reshape(b, m, A_HEADS, 2, HEAD_DIM)
    va_c = va_c.reshape(b, m, A_HEADS, A_VDIM)
    lam_init = 0.8 - 0.6 * math.exp(-0.3 * layer_idx)
    lam = (jnp.exp(jnp.sum(lam_q1.astype(jnp.float32) * lam_k1.astype(jnp.float32)))
           - jnp.exp(jnp.sum(lam_q2.astype(jnp.float32) * lam_k2.astype(jnp.float32))) + lam_init)
    k_all = jnp.concatenate([ka, ka_c], axis=1)
    v_all = jnp.concatenate([va, va_c], axis=1)
    q_blocks = qa.reshape(b, n // Q_BLOCK, Q_BLOCK, A_HEADS, 2, HEAD_DIM).swapaxes(0, 1)
    o_a = lax.map(lambda qblk: differential_attention(qblk, k_all, v_all, lam), q_blocks)
    o_a = o_a.swapaxes(0, 1).reshape(b, n, A_HEADS, A_VDIM)
    o_a = (rmsnorm(o_a, subln_g) * (1.0 - lam_init)).reshape(b, n, A_WIDTH)
    kb_c = kb_c.reshape(b, m, B_HEADS, HEAD_DIM)
    vb_c = vb_c.reshape(b, m, B_HEADS, HEAD_DIM)
    o_b = neighbourhood_attention(qb.reshape(b, n, B_HEADS, HEAD_DIM), kb.reshape(b, n, B_HEADS, HEAD_DIM),
                                  vb.reshape(b, n, B_HEADS, HEAD_DIM), kb_c, vb_c, rpb)
    out = jnp.concatenate([o_a, o_b], axis=-1) @ w_out
    if not ctx_out:
        return out, None
    oc_a = differential_attention(qa_c.reshape(b, m, A_HEADS, 2, HEAD_DIM), ka_c, va_c, lam)
    oc_a = (rmsnorm(oc_a, subln_g) * (1.0 - lam_init)).reshape(b, m, A_WIDTH)
    oc_b = context_attention(qb_c.reshape(b, m, B_HEADS, HEAD_DIM), kb_c, vb_c)
    out_c = jnp.concatenate([oc_a, oc_b], axis=-1) @ w_out
    return out, out_c

def mixer_odd(h, hc, ctx_out, *, w_in, w_out, sinks, conv_w, conv_b, a_log_f, a_log_b,
              dt_bias_f, dt_bias_b, d_skip, gnorm_g):
    b, n, _ = h.shape
    m = hc.shape[1]
    sizes = (C_Q, C_KV, C_KV, D_XBC, D_INNER, 2 * D_HEADS)
    q, k, v, xbc, z, dt = split_cols(h @ w_in, sizes)
    q_c, k_c, v_c, xbc_c, z_c, dt_c = split_cols(hc @ w_in, sizes)
    cos, sin = axial_rope_tables(n)
    q = apply_rope(q.reshape(b, n, C_HEADS, HEAD_DIM), cos, sin).reshape(b, n, C_KV_HEADS, C_REP, HEAD_DIM)
    k = apply_rope(k.reshape(b, n, C_KV_HEADS, HEAD_DIM), cos, sin)
    v = v.reshape(b, n, C_KV_HEADS, HEAD_DIM)
    k_c = k_c.reshape(b, m, C_KV_HEADS, HEAD_DIM)
    v_c = v_c.reshape(b, m, C_KV_HEADS, HEAD_DIM)
    o_c = window_attention_with_sink(q, k, v, k_c, v_c, sinks)
    a_f = -jnp.exp(a_log_f.astype(jnp.float32)).reshape(D_GROUPS, D_HPG)
    a_b = -jnp.exp(a_log_b.astype(jnp.float32)).reshape(D_GROUPS, D_HPG)
    xs, bm, cm, dtf, dtb = ssd_prep(xbc, dt, conv_w, conv_b, dt_bias_f, dt_bias_b)
    xs_c, bm_c, cm_c, dtf_c, dtb_c = ssd_prep(xbc_c, dt_c, conv_w, conv_b, dt_bias_f, dt_bias_b)
    flip = lambda u: jnp.flip(u, axis=1)
    s0 = jnp.zeros((b, D_GROUPS, D_HPG, D_HEADDIM, D_STATE), jnp.float32)
    yc_f, sc_f = ssd_chunked(xs_c, dtf_c, a_f, bm_c, cm_c, s0, ctx_out)
    yc_b, sc_b = ssd_chunked(flip(xs_c), flip(dtb_c), a_b, flip(bm_c), flip(cm_c), s0, ctx_out)
    y_f, _ = ssd_chunked(xs, dtf, a_f, bm, cm, sc_f, True)
    y_b, _ = ssd_chunked(flip(xs), flip(dtb), a_b, flip(bm), flip(cm), sc_b, True)
    o_d = ssd_output(y_f + flip(y_b), xs, z, d_skip, gnorm_g).astype(h.dtype)
    out = jnp.concatenate([o_c, o_d], axis=-1) @ w_out
    if not ctx_out:
        return out, None
    oc_c = sink_attention(q_c.reshape(b, m, C_KV_HEADS, C_REP, HEAD_DIM), k_c, v_c, sinks)
    oc_d = ssd_output(yc_f + flip(yc_b), xs_c, z_c, d_skip, gnorm_g).astype(h.dtype)
    out_c = jnp.concatenate([oc_c, oc_d], axis=-1) @ w_out
    return out, out_c

def trunk_layer(x, ctx, c, c_ctx, common, mixer, ctx_out):
    w_mod, b_mod, g_pre_mix, g_post_mix, g_pre_ffn, g_post_ffn, w_router, w_gate, w_up, w_down = common
    sh1, sc1, gt1, sh2, sc2, gt2 = ada_modulation(c, w_mod, b_mod)
    csh1, csc1, cgt1, csh2, csc2, cgt2 = ada_modulation(c_ctx, w_mod, b_mod)
    h = rmsnorm(x, g_pre_mix) * (1 + sc1) + sh1
    hc = rmsnorm(ctx, g_pre_mix) * (1 + csc1) + csh1
    mix, mix_c = mixer(h, hc, ctx_out)
    x = x + gt1 * rmsnorm(mix, g_post_mix)
    h = rmsnorm(x, g_pre_ffn) * (1 + sc2) + sh2
    x = x + gt2 * rmsnorm(expert_choice_ffn(h, w_router, w_gate, w_up, w_down), g_post_ffn)
    if ctx_out:
        ctx = ctx + cgt1 * rmsnorm(mix_c, g_post_mix)
        hc = rmsnorm(ctx, g_pre_ffn) * (1 + csc2) + csh2
        ctx = ctx + cgt2 * rmsnorm(expert_choice_ffn(hc, w_router, w_gate, w_up, w_down), g_post_ffn)
    return x, ctx

def setup_inputs(seed: int = 0) -> dict:
    key = jax.random.key(seed)
    keys = list(jax.random.split(key, 64))
    d = D_MODEL

    def normal(shape, std):
        return jax.random.normal(keys.pop(), shape, jnp.float32) * std

    def gain(n):
        return 1.0 + normal((n,), 0.05)

    def dt_bias_init():
        u = jax.random.uniform(keys.pop(), (D_HEADS,), jnp.float32)
        dt = jnp.exp(u * (math.log(0.1) - math.log(0.001)) + math.log(0.001))
        return dt + jnp.log(-jnp.expm1(-dt))

    p = {}
    p['x'] = normal((BATCH, SEQ, d), 1.0)
    p['c'] = normal((BATCH, d), 1.0)
    p['ctx'] = normal((BATCH, CTX_LEN, d), 1.0)
    p['c_ctx'] = normal((d,), 1.0)

    def add_common(pre, in_width):
        p[pre + 'w_mod'] = normal((d, 6 * d), 0.5 * d ** -0.5)
        p[pre + 'b_mod'] = normal((6 * d,), 0.02)
        for name in ('g_pre_mix', 'g_post_mix', 'g_pre_ffn', 'g_post_ffn'):
            p[pre + name] = gain(d)
        p[pre + 'w_in'] = normal((d, in_width), d ** -0.5)
        p[pre + 'w_out'] = normal((MIX_WIDTH, d), MIX_WIDTH ** -0.5)

    def add_moe(pre):
        p[pre + 'w_router'] = normal((d, N_EXPERTS), d ** -0.5)
        p[pre + 'w_gate'] = normal((N_EXPERTS, d, EXPERT_FF), d ** -0.5)
        p[pre + 'w_up'] = normal((N_EXPERTS, d, EXPERT_FF), d ** -0.5)
        p[pre + 'w_down'] = normal((N_EXPERTS, EXPERT_FF, d), EXPERT_FF ** -0.5)

    add_common('l0_', EVEN_IN)
    p['l0_lam_q1'] = normal((HEAD_DIM,), 0.1)
    p['l0_lam_k1'] = normal((HEAD_DIM,), 0.1)
    p['l0_lam_q2'] = normal((HEAD_DIM,), 0.1)
    p['l0_lam_k2'] = normal((HEAD_DIM,), 0.1)
    p['l0_subln_g'] = gain(A_VDIM)
    p['l0_rpb'] = normal((B_HEADS, 2 * NA_ROWS - 1, 2 * NA_COLS - 1), 0.1)
    add_moe('l0_')

    add_common('l1_', ODD_IN)
    p['l1_sinks'] = normal((C_HEADS,), 0.5)
    p['l1_conv_w'] = normal((D_CONV, 1, D_XBC), D_CONV ** -0.5)
    p['l1_conv_b'] = normal((D_XBC,), 0.02)
    p['l1_a_log_f'] = jnp.log(jax.random.uniform(keys.pop(), (D_HEADS,), jnp.float32, 1.0, 16.0))
    p['l1_a_log_b'] = jnp.log(jax.random.uniform(keys.pop(), (D_HEADS,), jnp.float32, 1.0, 16.0))
    p['l1_dt_bias_f'] = dt_bias_init()
    p['l1_dt_bias_b'] = dt_bias_init()
    p['l1_d_skip'] = 1.0 + normal((D_HEADS,), 0.1)
    p['l1_gnorm_g'] = gain(D_INNER)
    add_moe('l1_')
    return p

def reference(x, c, ctx, c_ctx,
              l0_w_mod, l0_b_mod, l0_g_pre_mix, l0_g_post_mix, l0_g_pre_ffn, l0_g_post_ffn,
              l0_w_in, l0_w_out, l0_lam_q1, l0_lam_k1, l0_lam_q2, l0_lam_k2, l0_subln_g, l0_rpb,
              l0_w_router, l0_w_gate, l0_w_up, l0_w_down,
              l1_w_mod, l1_b_mod, l1_g_pre_mix, l1_g_post_mix, l1_g_pre_ffn, l1_g_post_ffn,
              l1_w_in, l1_w_out, l1_sinks, l1_conv_w, l1_conv_b, l1_a_log_f, l1_a_log_b,
              l1_dt_bias_f, l1_dt_bias_b, l1_d_skip, l1_gnorm_g,
              l1_w_router, l1_w_gate, l1_w_up, l1_w_down):
    commons = [
        (l0_w_mod, l0_b_mod, l0_g_pre_mix, l0_g_post_mix, l0_g_pre_ffn, l0_g_post_ffn,
         l0_w_router, l0_w_gate, l0_w_up, l0_w_down),
        (l1_w_mod, l1_b_mod, l1_g_pre_mix, l1_g_post_mix, l1_g_pre_ffn, l1_g_post_ffn,
         l1_w_router, l1_w_gate, l1_w_up, l1_w_down),
    ]
    mixers = [
        functools.partial(mixer_even, layer_idx=0, w_in=l0_w_in, w_out=l0_w_out,
                          lam_q1=l0_lam_q1, lam_k1=l0_lam_k1, lam_q2=l0_lam_q2, lam_k2=l0_lam_k2,
                          subln_g=l0_subln_g, rpb=l0_rpb),
        functools.partial(mixer_odd, w_in=l1_w_in, w_out=l1_w_out, sinks=l1_sinks,
                          conv_w=l1_conv_w, conv_b=l1_conv_b, a_log_f=l1_a_log_f, a_log_b=l1_a_log_b,
                          dt_bias_f=l1_dt_bias_f, dt_bias_b=l1_dt_bias_b, d_skip=l1_d_skip,
                          gnorm_g=l1_gnorm_g),
    ]
    for i in range(DEPTH):
        x, ctx = trunk_layer(x, ctx, c, c_ctx, commons[i], mixers[i], i < DEPTH - 1)
    return x


_drawn_inputs = setup_inputs


def setup_inputs(seed=0):
    import zlib

    import numpy as np

    out = dict(_drawn_inputs(seed))
    spreads = {}
    factors = {'l1_g_post_ffn': 4.029, 'l1_sinks': 8.0, 'l1_d_skip': 3.237}
    for name, (base, spread) in spreads.items():
        noise = np.random.default_rng([zlib.crc32(name.encode()), seed]).standard_normal(out[name].shape)
        drawn = base * np.exp(spread * noise) if base else spread * noise
        out[name] = __import__('jax').numpy.asarray(drawn.astype(out[name].dtype))
    for name, factor in factors.items():
        out[name] = (out[name] * factor).astype(out[name].dtype)
    return out
```

```python
from contextlib import ExitStack
import math

import concourse.bass as bass
from concourse import mybir

F32 = mybir.dt.float32
I32 = mybir.dt.int32
U32 = mybir.dt.uint32
ALU = mybir.AluOpType
ACT = mybir.ActivationFunctionType
AX = mybir.AxisListType

P = 128
BANK = 512
D = 1024
KD = D // P
SEQ, CTX = 1024, 256
NTX, NTC = SEQ // P, CTX // P
NT = NTX + NTC
ROWS = SEQ + CTX
EPS = 1e-6
NEG = -1e30
E = 16
CAPX, CAPC = 2 * SEQ // E, 2 * CTX // E
HD = 64
SCALE = HD ** -0.5


class Stage:

    def __init__(self, nc, name):
        self.nc, self.name, self.stack, self.sems = nc, name, ExitStack(), []

    def __enter__(self):
        return self

    def sb(self, name, shape, dt=F32):
        return self.stack.enter_context(self.nc.sbuf_tensor(f"{self.name}_{name}", shape, dt))

    def ps(self, name, shape, dt=F32):
        return self.stack.enter_context(self.nc.psum_tensor(f"{self.name}_{name}_ps", shape, dt))

    def sem(self, name):
        s = self.stack.enter_context(self.nc.semaphore(f"{self.name}_{name}"))
        self.sems.append(s)
        return s

    def pool_sem(self, K, name):
        return K.stack.enter_context(self.nc.semaphore(f"{self.name}_{name}"))

    def __exit__(self, failed, *_):
        if failed:
            return
        with self.nc.Block() as block:

            @block.sync
            def _(sp):
                for s in self.sems:
                    sp.sem_clear(s)

        self.stack.close()


class Link:

    def __init__(self, eng, sem):
        self.eng, self.sem, self.before, self.base, self.n = eng, sem, 0, 0, 0

    def __call__(self, ins):
        self.n += 1
        ins.then_inc(self.sem, 1)
        self.eng.wait_ge(self.sem, self.base + self.n)

    def turn(self, i, per):
        self.before, self.n, self.per = self.before + self.n, 0, per
        self.base = self.eng.snap(i * per + self.before)

    def over(self, turns):
        assert self.n == self.per, (self.n, self.per)
        self.before += turns * self.per
        self.base, self.n = self.before, 0


def after(eng, sem, value):
    if not isinstance(value, int) or value > 0:
        eng.wait_ge(sem, value)


def columns(ap):
    return ap.rearrange("(k p) -> p k", p=P)


def modulation(nc, c, c_ctx, x, ctx, layers, res):
    WIDTH = 6 * D
    CHUNKS = WIDTH // BANK
    with Stage(nc, "mod") as st:
        cond = st.sb("cond", [P, 2, KD])
        gate = st.sb("gate", [P, 2, KD])
        w = st.sb("w", [P, 2, KD, BANK])
        bias = st.sb("bias", [2, 2, WIDTH])
        rows = st.sb("rows", [2, 2, WIDTH])
        acc = [st.ps(f"acc{s}", [P, BANK]) for s in range(2)]
        cond_in, bias_in, exp_done, silu_done = (st.sem(n) for n in ("cond_in", "bias_in", "exp_done", "silu_done"))
        w_in = [st.sem(f"w_in{s}") for s in range(2)]
        acc_done, acc_free, rows_done, stored, copied, step = (
            st.sem(n) for n in ("acc_done", "acc_free", "rows_done", "stored", "copied", "step"))

        with nc.Block() as block:

            @block.sync
            def _(sp):
                sp.dma_start(cond[:, 0, :], columns(c[0])).then_inc(cond_in, 16)
                sp.dma_start(cond[:, 1, :], columns(c_ctx)).then_inc(cond_in, 16)
                for n, (w_mod, b_mod, _) in enumerate(layers):
                    w_rows = w_mod.rearrange("(k p) n -> p k n", p=P)
                    with sp.Fori(0, CHUNKS // 2) as i:
                        for s in range(2):
                            sp.wait_ge(acc_done, i * 2 + (n * CHUNKS + s + 1))
                            sp.dma_start(w[:, s], w_rows[:, :, bass.ds(i * (2 * BANK) + s * BANK, BANK)]).then_inc(w_in[s], 16)

            @block.scalar
            def _(act):
                act.dma_start(res[0:SEQ, :], x[0]).then_inc(copied, 16)
                act.dma_start(res[SEQ:ROWS, :], ctx[0]).then_inc(copied, 16)
                for n, (_, b_mod, _) in enumerate(layers):
                    act.dma_start(bias[:, n, :], b_mod.rearrange("(a n) -> a n", a=1).broadcast_to([2, WIDTH])).then_inc(bias_in, 16)
                act.wait_ge(cond_in, 32)
                nc.scalar.activation(gate[:], cond[:], ACT.Exp, scale=-1.0).then_inc(exp_done, 1)
                for n, (_, _, mod) in enumerate(layers):
                    act.wait_ge(rows_done, CHUNKS * (n + 1))
                    act.dma_start(mod, rows[:, n, :]).then_inc(stored, 16)
                act.wait_ge(stored, 32)
                act.wait_ge(copied, 32)

            @block.tensor
            def _(pe):
                pe.sem_inc(acc_done, 2)
                pe.wait_ge(silu_done, 1)
                for n in range(len(layers)):
                    with pe.Fori(0, CHUNKS // 2) as i:
                        for s in range(2):
                            pe.wait_ge(w_in[s], i * 16 + 16 * (n * CHUNKS // 2 + 1))
                            pe.wait_ge(acc_free, i * 2 + (n * CHUNKS + s + 1))
                            for k in range(KD):
                                mm = nc.tensor.matmul(acc[s][0:2, :], gate[:, :, k], w[:, s, k, :], start=(k == 0), stop=(k == KD - 1))
                            mm.then_inc(acc_done, 1)

            @block.vector
            def _(dve):
                link = Link(dve, step)
                dve.sem_inc(acc_free, 2)
                dve.wait_ge(exp_done, 1)
                link(nc.vector.tensor_scalar(gate[:], gate[:], 1.0, None, ALU.add))
                link(nc.vector.reciprocal(gate[:], gate[:]))
                nc.vector.tensor_tensor(gate[:], gate[:], cond[:], ALU.mult).then_inc(silu_done, 1)
                dve.wait_ge(bias_in, 32)
                for n in range(len(layers)):
                    with dve.Fori(0, CHUNKS // 2) as i:
                        for s in range(2):
                            at = bass.ds(i * (2 * BANK) + s * BANK, BANK)
                            dve.wait_ge(acc_done, i * 2 + (n * CHUNKS + s + 3))
                            nc.vector.tensor_tensor(rows[:, n, at], acc[s][0:2, :], bias[:, n, at], ALU.add).then_inc(rows_done, 1)
                            dve.wait_ge(rows_done, i * 2 + (n * CHUNKS + s + 1))
                            dve.sem_inc(acc_free, 1)


def project(nc, name, K, res, mod, g_pre, w_in, proj):
    W = w_in.shape[1]
    WHOLE, REST = W // BANK, W % BANK
    with Stage(nc, name) as st:
        xt = st.sb("xt", [P, 2, D])
        xn = st.sb("xn", [P, 2, D])
        sq = st.sb("sq", [P, D])
        ms = st.sb("ms", [P, NT])
        rstd = st.sb("rstd", [P, NT])
        g = st.sb("g", [P, KD])
        shift = st.sb("shift", [P, 2, KD])
        gain = st.sb("gain", [P, 2, KD])
        hT = st.sb("hT", [P, KD, ROWS])
        w = st.sb("w", [P, 2, KD, BANK])
        ob = st.sb("ob", [P, 4, BANK])
        tp = [[st.ps(f"tp{s}{h}", [P, 4, P]) for h in range(2)] for s in range(2)]
        pb = [st.ps(f"pb{s}", [P, BANK]) for s in range(4)]
        vec_in, gain_done, ms_done, rstd_done, xn_done, tp_done, hv_done, ha_done, mm_done = (
            st.sem(n) for n in ("vec_in", "gain_done", "ms_done", "rstd_done", "xn_done", "tp_done", "hv_done", "ha_done", "mm_done"))
        xt_in = [st.sem(f"xt_in{s}") for s in range(2)]
        w_sem = [st.sem(f"w_in{s}") for s in range(2)]
        pool_step = st.sem("pool_step")
        out_done = [st.sem(f"out_done{s}") for s in range(2)]
        stored = [st.sem(f"stored{s}") for s in range(4)]
        w_rows = w_in.rearrange("(k p) n -> p k n", p=P)

        with nc.Block() as block:

            @block.sync
            def _(sp):
                for r in range(2):
                    sp.dma_start(shift[:, r, :], columns(mod[r, 0:D])).then_inc(vec_in, 16)
                    sp.dma_start(gain[:, r, :], columns(mod[r, D:2 * D])).then_inc(vec_in, 16)
                sp.dma_start(g[:], columns(g_pre)).then_inc(vec_in, 16)
                for t in range(NT):
                    if t >= 2:
                        sp.wait_ge(xn_done, t - 1)
                    sp.dma_start(xt[:, t % 2], res[t * P:(t + 1) * P, :]).then_inc(xt_in[t % 2], 16)
                with sp.Fori(0, WHOLE // 2) as i:
                    for s in range(2):
                        sp.wait_ge(mm_done, i * (2 * NT) + s * NT)
                        sp.dma_start(w[:, s], w_rows[:, :, bass.ds(i * (2 * BANK) + s * BANK, BANK)]).then_inc(w_sem[s], 16)
                if REST:
                    sp.wait_ge(mm_done, WHOLE * NT)
                    sp.dma_start(w[:, 0, :, 0:REST], w_rows[:, :, WHOLE * BANK:W]).then_inc(w_sem[0], 16)

            @block.gpsimd
            def _(pool):
                link = Link(pool, pool_step)
                for t in range(NT):
                    pool.wait_ge(ms_done, t + 1)
                    link(nc.gpsimd.tensor_scalar(rstd[:, t:t + 1], ms[:, t:t + 1], EPS, None, ALU.add))
                    nc.gpsimd.tensor_tensor(rstd[:, t:t + 1], rstd[:, t:t + 1], K.neg_half[:, 0:1], ALU.pow).then_inc(rstd_done, 1)

            @block.scalar
            def _(act):
                act.sem_inc(out_done[1], 1)

                def evacuate(t):
                    act.wait_ge(tp_done, t + 1)
                    for k in range(4, KD):
                        a = nc.scalar.activation(hT[:, k, t * P:(t + 1) * P], tp[t % 2][1][:, k - 4, :], ACT.Identity,
                                                 bias=shift[:, t // NTX, k:k + 1], scale=gain[:, t // NTX, k:k + 1])
                    a.then_inc(ha_done, 1)

                act.wait_ge(gain_done, 2)
                for t in range(NT):
                    act.wait_ge(xt_in[t % 2], 16 * (t // 2 + 1))
                    nc.scalar.activation(sq[:], xt[:, t % 2], ACT.Square, scale=D ** -0.5, accum_out=ms[:, t:t + 1]).then_inc(ms_done, 1)
                    if t >= 1:
                        evacuate(t - 1)
                    act.wait_ge(rstd_done, t + 1)
                    if t >= 2:
                        act.wait_ge(tp_done, t - 1)
                    nc.scalar.activation(xn[:, t % 2], xt[:, t % 2], ACT.Copy, scale=rstd[:, t:t + 1]).then_inc(xn_done, 1)
                    act.wait_ge(ms_done, t + 1)
                evacuate(NT - 1)

                def store(i, m, width):
                    act.wait_ge(out_done[m % 2], i * NT + (m // 2 + 2))
                    t, at = m % NT, i * (2 * BANK) + m // NT * BANK
                    at = at if isinstance(at, int) else act.snap(at)
                    act.dma_start(proj[t * P:(t + 1) * P, bass.ds(at, width)], ob[:, m % 4, 0:width]).then_inc(stored[m % 4], 16)

                def out(i, tiles, width):
                    for m in range(1, tiles, 2):
                        act.wait_ge(stored[m % 4], i * (16 * NT // 2) + 16 * (m // 4))
                        act.wait_ge(mm_done, i * (2 * NT) + (m + 1 + NT))
                        nc.scalar.activation(ob[:, m % 4, 0:width], pb[m % 4][:, 0:width], ACT.Copy).then_inc(out_done[1], 1)
                        store(i, m - 1, width)
                        store(i, m, width)

                with act.Fori(0, WHOLE // 2) as i:
                    out(i, 2 * NT, BANK)
                if REST:
                    out(WHOLE // 2, NT, REST)
                for s in range(4):
                    act.wait_ge(stored[s], 16 * (WHOLE * NT // 4 + (len(range(s, NT, 4)) if REST else 0)))

            @block.tensor
            def _(pe):
                for t in range(NT):
                    pe.wait_ge(xn_done, t + 1)
                    if t >= 2:
                        pe.wait_ge(hv_done, t - 1)
                        pe.wait_ge(ha_done, t - 1)
                    for k in range(KD):
                        mm = nc.tensor.transpose(tp[t % 2][k // 4][:, k % 4, :], xn[:, t % 2, k * P:(k + 1) * P], K.ident[:])
                    mm.then_inc(tp_done, 1)
                pe.wait_ge(hv_done, NT)
                pe.wait_ge(ha_done, NT)
                pe.sem_inc(mm_done, NT)

                def multiply(i, tiles, width):
                    for m in range(tiles):
                        if m % NT == 0:
                            pe.wait_ge(w_sem[m // NT], i * 16 + 16)
                        pe.wait_ge(out_done[m % 2], i * NT + m // 2)
                        t = m % NT
                        for k in range(KD):
                            mm = nc.tensor.matmul(pb[m % 4][:, 0:width], hT[:, k, t * P:(t + 1) * P], w[:, m // NT, k, 0:width],
                                                  start=(k == 0), stop=(k == KD - 1))
                        mm.then_inc(mm_done, 1)

                with pe.Fori(0, WHOLE // 2) as i:
                    multiply(i, 2 * NT, BANK)
                if REST:
                    multiply(WHOLE // 2, NT, REST)

            @block.vector
            def _(dve):
                dve.sem_inc(out_done[0], 1)
                dve.wait_ge(vec_in, 16 * 5)
                for r in range(2):
                    nc.vector.scalar_tensor_tensor(gain[:, r, :], gain[:, r, :], 1.0, g[:], ALU.add, ALU.mult).then_inc(gain_done, 1)
                dve.wait_ge(gain_done, 2)
                for t in range(NT):
                    dve.wait_ge(tp_done, t + 1)
                    for k in range(4):
                        v = nc.vector.tensor_scalar(hT[:, k, t * P:(t + 1) * P], tp[t % 2][0][:, k, :], gain[:, t // NTX, k:k + 1],
                                                    shift[:, t // NTX, k:k + 1], ALU.mult, ALU.add)
                    v.then_inc(hv_done, 1)

                def out(i, tiles, width):
                    for m in range(0, tiles, 2):
                        dve.wait_ge(stored[m % 4], i * (16 * NT // 2) + 16 * (m // 4))
                        dve.wait_ge(mm_done, i * (2 * NT) + (m + 1 + NT))
                        nc.vector.tensor_copy(ob[:, m % 4, 0:width], pb[m % 4][:, 0:width]).then_inc(out_done[0], 1)

                with dve.Fori(0, WHOLE // 2) as i:
                    out(i, 2 * NT, BANK)
                if REST:
                    out(WHOLE // 2, NT, REST)


class Constants:

    def __init__(self, nc, stack):
        self.stack = stack
        self.ident = stack.enter_context(nc.sbuf_tensor("ident", [P, P], F32))
        self.neg_half = stack.enter_context(nc.sbuf_tensor("neg_half", [P, 16], F32))
        self.eps = stack.enter_context(nc.sbuf_tensor("eps", [P, 16], F32))
        with Stage(nc, "const") as st:
            filled = st.sem("filled")
            with nc.Block() as block:

                @block.gpsimd
                def _(pool):
                    nc.gpsimd.memset(self.neg_half[:], -0.5).then_inc(filled, 1)
                    nc.gpsimd.memset(self.eps[:], EPS).then_inc(filled, 1)
                    nc.gpsimd.memset(self.ident[:], 0.0).then_inc(filled, 1)
                    pool.wait_ge(filled, 3)
                    nc.gpsimd.affine_select(out=self.ident[:], in_=self.ident[:], compare_op=ALU.not_equal, fill=1.0,
                                            base=0, pattern=[[-1, P]], channel_multiplier=1).then_inc(filled, 1)
                    pool.wait_ge(filled, 4)



def rotate_pairs(nc, link, src, dst, cos, sin, t1, t2):
    pair = src[:, 0:NTX, :].rearrange("p t (n two) -> p t n two", two=2)
    to = dst[:].rearrange("p t (n two) -> p t n two", two=2)
    link(nc.gpsimd.tensor_tensor(t1[:], pair[:, :, :, 0], cos[:], ALU.mult))
    link(nc.gpsimd.tensor_tensor(t2[:], pair[:, :, :, 1], sin[:], ALU.mult))
    link(nc.gpsimd.tensor_tensor(to[:, :, :, 0], t1[:], t2[:], ALU.subtract))
    link(nc.gpsimd.tensor_tensor(t1[:], pair[:, :, :, 0], sin[:], ALU.mult))
    link(nc.gpsimd.tensor_tensor(t2[:], pair[:, :, :, 1], cos[:], ALU.mult))
    link(nc.gpsimd.tensor_tensor(to[:, :, :, 1], t1[:], t2[:], ALU.add))


def differential_attention(nc, K, proj, rope_cos, rope_sin, lam_vectors, subln_g, layer_idx, out):
    H = 4
    QK = H * 2 * HD
    LAM_INIT = 0.8 - 0.6 * math.exp(-0.3 * layer_idx)
    ROUNDS = NTX * 3 + NTC
    with Stage(nc, "attn_a") as st:
        q = st.sb("q", [P, NT, P])
        k = st.sb("k", [P, NT, P])
        v = st.sb("v", [P, NT, P])
        qr = st.sb("qr", [P, NTX, P])
        kr = st.sb("kr", [P, NTX, P])
        cos = st.sb("cos", [P, NTX, HD])
        sin = st.sb("sin", [P, NTX, HD])
        t1 = st.sb("t1", [P, NTX, HD])
        t2 = st.sb("t2", [P, NTX, HD])
        qT = st.sb("qT", [P, ROWS])
        kT = st.sb("kT", [P, ROWS])
        e = st.sb("e", [P, 2, ROWS])
        a = st.sb("a", [P, 2, ROWS])
        aT = st.sb("aT", [P, NT, P])
        ob = st.sb("ob", [P, NT, P])
        sq = st.sb("sq", [P, P])
        ms = st.sb("ms", [P, NT])
        g = st.sb("g", [P, P])
        lv = st.sb("lv", [P, 4, HD])
        lp = st.sb("lp", [P, 2, HD])
        ls = st.sb("ls", [P, 2])
        nlam = st.sb("nlam", [P, 1])
        nmx = st.sb("nmx", [P, 2])
        sums = st.sb("sums", [P, 2])
        r = st.sb("r", [P, 2])
        S = [st.ps(f"s{m}", [P, 3 * BANK]) for m in range(2)]
        T = st.ps("t", [P, 4, P])
        O = st.ps("o", [P, BANK])
        (const_in, q_in, k_in, v_in, rope_done, prep_done, qt_done, kt_done, mx_done, r_done, e1_done, a_done,
         t_done, t_out, o_done, o_out, lam_exp, dve_step, act_step, pool_step) = (st.sem(n) for n in (
             "const_in q_in k_in v_in rope_done prep_done qt_done kt_done mx_done r_done e1_done a_done "
             "t_done t_out o_done o_out lam_exp dve_step act_step pool_step").split())
        stored = st.pool_sem(K, "stored")
        s_done = [st.sem(f"s_done{m}") for m in range(2)]
        exp_done = [st.sem(f"exp_done{m}") for m in range(2)]
        rows = proj.rearrange("(t p) n -> p t n", p=P)

        def keys(t):
            return (0, ROWS) if t < NTX else (SEQ, CTX)

        def rounds(t):
            first, n = (0, NT) if t < NTX else (NTX, NTC)
            return [list(range(j, min(j + 4, first + n))) for j in range(first, first + n, 4)]

        def round_at(t):
            return 3 * min(t, NTX) + max(t - NTX, 0)

        with nc.Block() as block:

            @block.sync
            def _(sp):
                sp.dma_start(cos[:], rope_cos.rearrange("(t p) n -> p t n", p=P)).then_inc(const_in, 16)
                sp.dma_start(sin[:], rope_sin.rearrange("(t p) n -> p t n", p=P)).then_inc(const_in, 16)
                sp.dma_start(g[:], subln_g.rearrange("(a n) -> a n", a=1).broadcast_to([P, P])).then_inc(const_in, 16)
                for j, vec in enumerate(lam_vectors):
                    sp.dma_start(lv[:, j, :], vec.rearrange("(a n) -> a n", a=1).broadcast_to([P, HD])).then_inc(const_in, 16)
                with sp.Fori(0, H) as h:
                    sp.wait_ge(prep_done, h)
                    sp.dma_start(q[:], rows[:, :, bass.ds(h * P, P)]).then_inc(q_in, 16)
                    sp.dma_start(k[:], rows[:, :, bass.ds(h * P + QK, P)]).then_inc(k_in, 16)
                    sp.wait_ge(o_done, h * NT)
                    sp.dma_start(v[:], rows[:, :, bass.ds(h * P + 2 * QK, P)]).then_inc(v_in, 16)

            @block.gpsimd
            def _(pool):
                link = Link(pool, pool_step)

                def rotate(h):
                    for src, dst, loaded in ((q, qr, q_in), (k, kr, k_in)):
                        pool.wait_ge(loaded, h * 16 + 16)
                        after(pool, prep_done, h)
                        rotate_pairs(nc, link, src, dst, cos, sin, t1, t2)
                        pool.sem_inc(rope_done, 1)

                def normalise(h):
                    pool.wait_ge(o_out, h * NT + NT)
                    link(nc.gpsimd.tensor_tensor(ms[:], ms[:], K.eps[:, 0:NT], ALU.add))
                    link(nc.gpsimd.tensor_tensor(ms[:], ms[:], K.neg_half[:, 0:NT], ALU.pow))
                    link(nc.gpsimd.tensor_tensor(ob[:], ob[:], ms[:].unsqueeze(2).to_broadcast([P, NT, P]), ALU.mult))
                    link(nc.gpsimd.tensor_tensor(ob[:], ob[:], g[:].unsqueeze(1).to_broadcast([P, NT, P]), ALU.mult))
                    at = h * P if isinstance(h, int) else pool.snap(h * P)
                    pool.dma_start(out.rearrange("(t p) n -> p t n", p=P)[:, :, bass.ds(at, P)], ob[:]).then_inc(stored, 16)

                pool.wait_ge(const_in, 16 * 7)
                link(nc.gpsimd.tensor_scalar(g[:], g[:], 1.0 - LAM_INIT, None, ALU.mult))
                rotate(0)
                with pool.Fori(1, H) as h:
                    link.turn(h - 1, 16)
                    rotate(h)
                    normalise(h - 1)
                link.over(H - 1)
                normalise(H - 1)
                pool.wait_ge(stored, 16 * H)

            @block.scalar
            def _(act):
                link = Link(act, act_step)
                act.wait_ge(dve_step, 2)
                nc.scalar.activation(ls[:], ls[:], ACT.Exp).then_inc(lam_exp, 1)

                def exp(h, t, m):
                    first, n = keys(t)
                    act.wait_ge(mx_done, h * (2 * NT) + (2 * t + m + 1))
                    act.wait_ge(a_done, h * NT + t)
                    nc.scalar.activation(e[:, m, 0:n], S[m][:, 0:n], ACT.Exp, bias=nmx[:, m:m + 1],
                                         accum_out=sums[:, m:m + 1]).then_inc(exp_done[m], 1)

                def weigh(h, t):
                    n = keys(t)[1]
                    act.wait_ge(r_done, h * NT + (t + 1))
                    nc.scalar.activation(e[:, 1, 0:n], e[:, 1, 0:n], ACT.Copy, scale=r[:, 1:2]).then_inc(e1_done, 1)

                def transposed(h, t, j):
                    if j < len(rounds(t)):
                        tiles = rounds(t)[j]
                        act.wait_ge(t_done, h * ROUNDS + (round_at(t) + j + 1))
                        nc.scalar.activation(aT[:, tiles[0]:tiles[-1] + 1, :], T[:, 0:len(tiles), :], ACT.Copy).then_inc(t_out, 1)

                def output(h, t):
                    act.wait_ge(o_done, h * NT + (t + 1))
                    if t == 0:
                        act.wait_ge(stored, h * 16)
                    link(nc.scalar.activation(ob[:, t, :], O[:, 0:P], ACT.Copy))
                    link(nc.scalar.activation(sq[:], O[:, 0:P], ACT.Square, scale=P ** -0.5, accum_out=ms[:, t:t + 1]))
                    act.sem_inc(o_out, 1)

                with act.Fori(0, H) as h:
                    link.turn(h, 2 * NT)
                    act.wait_ge(prep_done, h + 1)
                    nc.scalar.activation(kT[:], S[1][:, 0:ROWS], ACT.Copy).then_inc(kt_done, 1)
                    exp(h, 0, 0)
                    exp(h, 0, 1)
                    weigh(h, 0)
                    for t in range(1, NT + 1):
                        if t < NT:
                            exp(h, t, 0)
                        transposed(h, t - 1, 0)
                        if t < NT:
                            exp(h, t, 1)
                        transposed(h, t - 1, 1)
                        if t < NT:
                            weigh(h, t)
                        transposed(h, t - 1, 2)
                        output(h, t - 1)
                link.over(H)

            @block.vector
            def _(dve):
                link = Link(dve, dve_step)
                dve.wait_ge(const_in, 16 * 7)
                link(nc.vector.tensor_tensor(lp[:], lv[:, 0:4:2, :], lv[:, 1:4:2, :], ALU.mult))
                link(nc.vector.tensor_reduce(ls[:], lp[:], AX.X, ALU.add))
                dve.wait_ge(lam_exp, 1)
                link(nc.vector.tensor_tensor(nlam[:], ls[:, 1:2], ls[:, 0:1], ALU.subtract))
                link(nc.vector.tensor_scalar(nlam[:], nlam[:], -LAM_INIT, None, ALU.add))
                with dve.Fori(0, H) as h:
                    link.turn(h, NT)
                    dve.wait_ge(prep_done, h + 1)
                    nc.vector.tensor_scalar(qT[:], S[0][:, 0:ROWS], SCALE, None, ALU.mult).then_inc(qt_done, 1)
                    for t in range(NT):
                        n = keys(t)[1]
                        for m in range(2):
                            dve.wait_ge(s_done[m], h * NT + (t + 1))
                            nc.vector.tensor_reduce(nmx[:, m:m + 1], S[m][:, 0:n], AX.X, ALU.max, negate=True).then_inc(mx_done, 1)
                        for m in range(2):
                            dve.wait_ge(exp_done[m], h * NT + (t + 1))
                        link(nc.vector.reciprocal(r[:], sums[:]))
                        nc.vector.tensor_tensor(r[:, 1:2], r[:, 1:2], nlam[:], ALU.mult).then_inc(r_done, 1)
                        dve.wait_ge(e1_done, h * NT + (t + 1))
                        nc.vector.scalar_tensor_tensor(a[:, t % 2, 0:n], e[:, 0, 0:n], r[:, 0:1], e[:, 1, 0:n],
                                                       ALU.mult, ALU.add).then_inc(a_done, 1)
                link.over(H)

            @block.tensor
            def _(pe):
                def score(h, t, m):
                    first, n = keys(t)
                    pe.wait_ge(exp_done[m], h * NT + t)
                    for c in range(0, n, BANK):
                        w = min(BANK, n - c)
                        mm = nc.tensor.matmul(S[m][:, c:c + w], qT[m * HD:(m + 1) * HD, t * P:(t + 1) * P],
                                              kT[m * HD:(m + 1) * HD, first + c:first + c + w], start=True, stop=True)
                    mm.then_inc(s_done[m], 1)

                def turn_round(h, t, j):
                    first = keys(t)[0]
                    if j == 0:
                        pe.wait_ge(a_done, h * NT + (t + 1))
                    pe.wait_ge(t_out, h * ROUNDS + (round_at(t) + j))
                    for i, kt in enumerate(rounds(t)[j]):
                        c = kt * P - first
                        mm = nc.tensor.transpose(T[:, i, :], a[:, t % 2, c:c + P], K.ident[:])
                    mm.then_inc(t_done, 1)

                def weigh_values(h, t, j):
                    pe.wait_ge(t_out, h * ROUNDS + (round_at(t) + j + 1))
                    if j == 0:
                        pe.wait_ge(o_out, h * NT + t)
                    last = rounds(t)[-1][-1]
                    for kt in rounds(t)[j]:
                        mm = nc.tensor.matmul(O[:, 0:P], aT[:, kt, :], v[:, kt, :], start=(kt * P == keys(t)[0]), stop=(kt == last))
                    if j == len(rounds(t)) - 1:
                        mm.then_inc(o_done, 1)

                with pe.Fori(0, H) as h:
                    pe.wait_ge(rope_done, h * 2 + 2)
                    for m, (src, raw) in enumerate(((qr, q), (kr, k))):
                        pe.wait_ge(exp_done[m], h * NT)
                        for t in range(NT):
                            mm = nc.tensor.transpose(S[m][:, t * P:(t + 1) * P], (src if t < NTX else raw)[:, t, :], K.ident[:])
                    mm.then_inc(prep_done, 1)
                    pe.wait_ge(qt_done, h + 1)
                    pe.wait_ge(kt_done, h + 1)
                    score(h, 0, 0)
                    score(h, 0, 1)
                    for t in range(NT):
                        if t + 1 < NT:
                            score(h, t + 1, 0)
                            score(h, t + 1, 1)
                        if t == 0:
                            pe.wait_ge(v_in, h * 16 + 16)
                        n = len(rounds(t))
                        turn_round(h, t, 0)
                        for j in range(1, n):
                            turn_round(h, t, j)
                            weigh_values(h, t, j - 1)
                        weigh_values(h, t, n - 1)



def local_attention(nc, K, kind, proj, out, rope=None, rpb=None, sinks=None, scratch=None):
    near = kind == "near"
    TURNS = 4
    NL = 5 if near else 3
    W = NL * P + CTX
    NQ = NT if near else NTX
    NS = 2 * NQ
    CLASSES = 5 if near else 3
    HEADS = 2 if near else 1
    GRID = 64
    LINE, BIASES = 96, 8 * 15
    Q0, K0, V0 = (1536, 2048, 2560) if near else (0, 512, 640)

    def start(t):
        return min(max(t - NL // 2, 0), NTX - NL)

    def bias_class(t):
        if t >= NTX:
            return 0
        return {0: 0, 1: 1, 6: 3, 7: 4}.get(t, 2) if near else {0: 0, 7: 2}.get(t, 1)

    def span(t):
        return (0, W) if t < NTX else (NL * P, W)

    def tiles(t):
        seen = [(c * P, start(t) + c) for c in range(NL)] if t < NTX else []
        seen += [(NL * P + c * P, NTX + c) for c in range(NTC)]
        n = (len(seen) + 1) // 2
        return seen[:n], seen[n:]

    with Stage(nc, "attn_" + kind) as st:
        q = st.sb("q", [P, NT, P])
        k = st.sb("k", [P, NT, P])
        v = st.sb("v", [P, NT, P])
        qT = st.sb("qT", [P, ROWS])
        kT = st.sb("kT", [P, ROWS])
        bias = st.sb("bias", [P, HEADS, CLASSES, W])
        sb = st.sb("sb", [P, 2, W])
        aT = st.sb("aT", [P, 8, P])
        ob = st.sb("ob", [P, NQ, P])
        nmx = st.sb("nmx", [P, 4])
        sums = st.sb("sums", [P, 4])
        r = st.sb("r", [P, 4])
        S = [st.ps(f"s{s}", [P, 2 * BANK]) for s in range(2)]
        T = [st.ps(f"tr{s}", [P, 4, P]) for s in range(2)]
        O = [st.ps(f"o{s}", [P, BANK]) for s in range(2)]
        (q_in, k_in, v_in, bias_in, ready, prep_done, qt_done, kt_done, s_done, b_done, mx_done, exp_done, r_done,
         t_done, tv_out, ta_out, o_done, o_out, stored, dve_step, act_step, pool_step, const_in) = (st.sem(n) for n in (
             "q_in k_in v_in bias_in ready prep_done qt_done kt_done s_done b_done mx_done exp_done r_done "
             "t_done tv_out ta_out o_done o_out stored dve_step act_step pool_step const_in").split())
        rows = proj.rearrange("(t p) n -> p t n", p=P)
        if near:
            win = st.sb("win", [GRID, BIASES, GRID])
            mask = st.sb("mask", [GRID, GRID])
            skewed, lines = scratch
            zeros = st.sb("zeros", [GRID, BIASES * LINE + 1])
            PARTS = [(h2, cls, a) for h2 in range(2) for cls in range(CLASSES) for a in range(2)]
        else:
            qr = st.sb("qr", [P, NTX, P])
            kr = st.sb("kr", [P, NTX, P])
            cos = st.sb("cos", [P, NTX, HD])
            sin = st.sb("sin", [P, NTX, HD])
            t1 = st.sb("t1", [P, NTX, HD])
            t2 = st.sb("t2", [P, NTX, HD])
            sink = st.sb("sink", [P, 2, TURNS])
            nsink = st.sb("nsink", [P, 2, TURNS])
            sk = st.sb("sk", [P, 2])
            nsk = st.sb("nsk", [P, 2])
            es = st.sb("es", [P, 4])
            sink_done = st.sem("sink_done")

        def bias_rows(cls, a):
            t = {0: 0, 1: 1, 2: 2, 3: 6, 4: 7}[cls]
            row = 2 * t + a
            first = min(max(row - 4, 0), 8)
            return first - 2 * start(t), first - row + 7

        with nc.Block() as block:

            @block.sync
            def _(sp):
                if near:
                    sp.wait_ge(ready, 1)
                    sp.dma_start(skewed.rearrange("(w n) -> w n", w=GRID), zeros[:]).then_inc(const_in, 16)
                    sp.wait_ge(const_in, 16)
                    sp.dma_start(
                        skewed.rearrange("(w n) -> w n", w=GRID)[:, 0:BIASES * LINE].rearrange("w (b l) -> w b l", l=LINE)[:, :, 0:31],
                        rpb.rearrange("h r c -> (h r) c").unsqueeze(0).broadcast_to([GRID, BIASES, 31])).then_inc(const_in, 16)
                    sp.wait_ge(const_in, 32)
                    sp.dma_start(win[:], skewed[0:GRID * BIASES * LINE].rearrange("(w b l) -> w b l", w=GRID, l=LINE)[:, :, 15:15 + GRID]).then_inc(const_in, 16)
                    sp.wait_ge(ready, 2)
                    sp.dma_start(lines, win[:].rearrange("w b c -> w (b c)")).then_inc(const_in, 16)
                    sp.wait_ge(const_in, 64)
                else:
                    sp.dma_start(cos[:], rope[0].rearrange("(t p) n -> p t n", p=P)).then_inc(const_in, 16)
                    sp.dma_start(sin[:], rope[1].rearrange("(t p) n -> p t n", p=P)).then_inc(const_in, 16)
                    sp.dma_start(sink[:], sinks.rearrange("(a h j) -> a h j", a=1, h=2).broadcast_to([P, 2, TURNS])).then_inc(const_in, 16)
                with sp.Fori(0, TURNS) as i:
                    sp.wait_ge(prep_done, i)
                    if near:
                        sp.dma_start(q[:], rows[:, :, bass.ds(i * P + Q0, P)]).then_inc(q_in, 16)
                        sp.dma_start(k[:], rows[:, :, bass.ds(i * P + K0, P)]).then_inc(k_in, 16)
                        sp.wait_ge(b_done, i * NS)
                        for h2, cls, a in PARTS:
                            at, rel = bias_rows(cls, a)
                            sp.dma_start(bias[a * GRID:(a + 1) * GRID, h2, cls, at * GRID:(at + 8) * GRID],
                                         lines[:, bass.ds(i * (2 * 15 * GRID) + (h2 * 15 + rel) * GRID, 8 * GRID)]).then_inc(bias_in, 16)
                        sp.wait_ge(o_done, i * NS)
                        sp.dma_start(v[:], rows[:, :, bass.ds(i * P + V0, P)]).then_inc(v_in, 16)
                    else:
                        for h2 in range(2):
                            sp.dma_start(q[:, :, h2 * HD:(h2 + 1) * HD], rows[:, :, bass.ds(i * HD + Q0 + h2 * TURNS * HD, HD)]).then_inc(q_in, 16)
                        sp.dma_start(k[:], rows[:, :, K0:K0 + P]).then_inc(k_in, 16)
                        sp.wait_ge(o_done, i * NS)
                        sp.dma_start(v[:], rows[:, :, V0:V0 + P]).then_inc(v_in, 16)

            @block.gpsimd
            def _(pool):
                link = Link(pool, pool_step)
                if near:
                    link(nc.gpsimd.memset(zeros[:], 0.0))
                    pool.sem_inc(ready, 1)
                    link(nc.gpsimd.memset(mask[:], 0.0))
                    link(nc.gpsimd.affine_select(out=mask[:, 0:48], in_=mask[:, 0:48], compare_op=ALU.is_ge, fill=NEG,
                                                 base=8, pattern=[[1, 48]], channel_multiplier=-1))
                    link(nc.gpsimd.affine_select(out=mask[:, 16:64], in_=mask[:, 16:64], compare_op=ALU.is_ge, fill=NEG,
                                                 base=7 - 16, pattern=[[-1, 48]], channel_multiplier=1))
                    link(nc.gpsimd.memset(bias[:, :, :, 0:NL * P], NEG))
                    link(nc.gpsimd.memset(bias[:, :, :, NL * P:W], 0.0))
                    pool.wait_ge(const_in, 48)
                    link(nc.gpsimd.tensor_tensor(win[:], win[:], mask[:].unsqueeze(1).to_broadcast([GRID, BIASES, GRID]), ALU.add))
                    pool.sem_inc(ready, 1)
                else:
                    link(nc.gpsimd.memset(bias[:], 0.0))

                    def after_query(cls, c):
                        link(nc.gpsimd.affine_select(out=bias[:, 0, cls, c * P:(c + 1) * P], in_=bias[:, 0, cls, c * P:(c + 1) * P],
                                                     compare_op=ALU.is_ge, fill=NEG, base=0, pattern=[[-1, P]], channel_multiplier=1))

                    def before_query(cls, c):
                        link(nc.gpsimd.affine_select(out=bias[:, 0, cls, c * P:(c + 1) * P], in_=bias[:, 0, cls, c * P:(c + 1) * P],
                                                     compare_op=ALU.is_ge, fill=NEG, base=0, pattern=[[1, P]], channel_multiplier=-1))

                    after_query(0, 1)
                    link(nc.gpsimd.memset(bias[:, 0, 0, 2 * P:3 * P], NEG))
                    before_query(1, 0)
                    after_query(1, 2)
                    link(nc.gpsimd.memset(bias[:, 0, 2, 0:P], NEG))
                    before_query(2, 1)
                    pool.wait_ge(const_in, 48)
                    link(nc.gpsimd.tensor_scalar(nsink[:], sink[:], -1.0, None, ALU.mult))
                    pool.sem_inc(ready, 1)
                    with pool.Fori(0, TURNS) as i:
                        link.turn(i, 12)
                        pool.wait_ge(q_in, i * 32 + 32)
                        pool.wait_ge(prep_done, i)
                        rotate_pairs(nc, link, q, qr, cos, sin, t1, t2)
                        pool.wait_ge(k_in, i * 16 + 16)
                        rotate_pairs(nc, link, k, kr, cos, sin, t1, t2)
                        pool.sem_inc(ready, 1)
                    link.over(TURNS)

            @block.scalar
            def _(act):
                link = Link(act, act_step)
                act.sem_inc(o_out, 1)

                def exp(i, s):
                    h2, t = divmod(s, NQ)
                    first, end = span(t)
                    act.wait_ge(mx_done, i * NS + (s + 1))
                    nc.scalar.activation(sb[:, s % 2, first:end], sb[:, s % 2, first:end], ACT.Exp, bias=nmx[:, s % 4:s % 4 + 1],
                                         accum_out=sums[:, s % 4:s % 4 + 1]).then_inc(exp_done, 1)
                    if not near:
                        nc.scalar.activation(es[:, s % 4:s % 4 + 1], sk[:, h2:h2 + 1], ACT.Exp,
                                             bias=nmx[:, s % 4:s % 4 + 1]).then_inc(sink_done, 1)

                def transposed(i, s):
                    half = tiles(s % NQ)[1]
                    act.wait_ge(t_done, i * NS + (s + 1))
                    nc.scalar.activation(aT[:, 4:4 + len(half), :], T[1][:, 0:len(half), :], ACT.Copy).then_inc(ta_out, 1)

                def output(i, s):
                    h2, t = divmod(s, NQ)
                    act.wait_ge(o_done, i * NS + (s + 1))
                    act.wait_ge(r_done, i * NS + (s + 1))
                    if s == 0:
                        act.wait_ge(stored, i * (16 if near else 32))
                    nc.scalar.activation(ob[:, t, h2 * HD:(h2 + 1) * HD], O[s % 2][:, 0:HD], ACT.Copy,
                                         scale=r[:, s % 4:s % 4 + 1]).then_inc(o_out, 1)

                with act.Fori(0, TURNS) as i:
                    act.wait_ge(prep_done, i + 1)
                    link.turn(i, 1)
                    link(nc.scalar.activation(kT[:, 0:8 * P], S[1][:], ACT.Copy))
                    nc.scalar.activation(kT[:, 8 * P:ROWS].rearrange("p (a b) -> p a b", a=2), T[1][:, 0:2, :], ACT.Copy).then_inc(kt_done, 1)
                    for s in range(NS + 2):
                        if s < NS:
                            exp(i, s)
                        if 1 <= s <= NS:
                            transposed(i, s - 1)
                        if s >= 2:
                            output(i, s - 2)
                    act.wait_ge(o_out, i * NS + (NS + 1))
                    to = out.rearrange("(t p) n -> p t n", p=P)[:, 0:NQ, :]
                    if near:
                        at = act.snap(i * P + BANK)
                        act.dma_start(to[:, :, bass.ds(at, P)], ob[:]).then_inc(stored, 16)
                    else:
                        at = act.snap(i * HD)
                        for h2 in range(2):
                            act.dma_start(to[:, :, bass.ds(at + h2 * TURNS * HD, HD)], ob[:, :, h2 * HD:(h2 + 1) * HD]).then_inc(stored, 16)
                link.over(TURNS)
                act.wait_ge(stored, TURNS * (16 if near else 32))

            @block.vector
            def _(dve):
                link = Link(dve, dve_step)

                def scores(i, s):
                    h2, t = divmod(s, NQ)
                    first, end = span(t)
                    at = s % 4
                    dve.wait_ge(s_done, i * NS + (s + 1))
                    nc.vector.tensor_tensor(sb[:, s % 2, first:end], S[s % 2][:, first:end],
                                            bias[:, h2 % HEADS, bias_class(t), first:end], ALU.add).then_inc(b_done, 1)
                    dve.wait_ge(b_done, i * NS + (s + 1))
                    red = nc.vector.tensor_reduce(nmx[:, at:at + 1], sb[:, s % 2, first:end], AX.X, ALU.max, negate=True)
                    if near:
                        red.then_inc(mx_done, 1)
                    else:
                        link(red)
                        nc.vector.tensor_tensor(nmx[:, at:at + 1], nmx[:, at:at + 1], nsk[:, h2:h2 + 1], ALU.min).then_inc(mx_done, 1)

                def rest(i, s):
                    at = s % 4
                    dve.wait_ge(exp_done, i * NS + (s + 1))
                    if not near:
                        dve.wait_ge(sink_done, i * NS + (s + 1))
                        link(nc.vector.tensor_tensor(sums[:, at:at + 1], sums[:, at:at + 1], es[:, at:at + 1], ALU.add))
                    nc.vector.reciprocal(r[:, at:at + 1], sums[:, at:at + 1]).then_inc(r_done, 1)
                    half = tiles(s % NQ)[0]
                    dve.wait_ge(t_done, i * NS + (s + 1))
                    nc.vector.tensor_copy(aT[:, 0:len(half), :], T[0][:, 0:len(half), :]).then_inc(tv_out, 1)

                if near:
                    dve.wait_ge(ready, 2)
                else:
                    dve.wait_ge(ready, 1)
                with dve.Fori(0, TURNS) as i:
                    link.turn(i, 1 if near else 1 + 2 + 2 * NS)
                    dve.wait_ge(prep_done, i + 1)
                    link(nc.vector.tensor_scalar(qT[:, 0:8 * P], S[0][:], SCALE, None, ALU.mult))
                    nc.vector.tensor_scalar(qT[:, 8 * P:ROWS].rearrange("p (a b) -> p a b", a=2), T[0][:, 0:2, :], SCALE, None, ALU.mult).then_inc(qt_done, 1)
                    if near:
                        dve.wait_ge(bias_in, i * (16 * len(PARTS)) + 16 * len(PARTS))
                    else:
                        link(nc.vector.tensor_copy(nsk[:], nsink[:, :, bass.ds(i, 1)].rearrange("p h j -> p (h j)")))
                        link(nc.vector.tensor_copy(sk[:], sink[:, :, bass.ds(i, 1)].rearrange("p h j -> p (h j)")))
                    for s in range(NS + 1):
                        if s < NS:
                            scores(i, s)
                        if s >= 1:
                            rest(i, s - 1)
                link.over(TURNS)

            @block.tensor
            def _(pe):
                def score(i, s):
                    h2, t = divmod(s, NQ)
                    if s >= 2:
                        pe.wait_ge(b_done, i * NS + (s - 1))
                    runs = [(NL * P, SEQ, CTX)] if t >= NTX else (
                        [(0, start(t) * P, min(NL * P, BANK))] + [(BANK, start(t) * P + BANK, NL * P - BANK)] * (NL * P > BANK)
                        + ([(NL * P, SEQ, CTX)] if NL * P >= BANK else [(NL * P, SEQ, BANK - NL * P), (BANK, SEQ + BANK - NL * P, W - BANK)]))
                    for to, first, n in runs:
                        mm = nc.tensor.matmul(S[s % 2][:, to:to + n], qT[h2 * HD:(h2 + 1) * HD, t * P:(t + 1) * P],
                                              kT[h2 * HD:(h2 + 1) * HD, first:first + n], start=True, stop=True)
                    mm.then_inc(s_done, 1)

                def turn_weights(i, s):
                    pe.wait_ge(exp_done, i * NS + (s + 1))
                    pe.wait_ge(tv_out, i * NS + s)
                    pe.wait_ge(ta_out, i * NS + s)
                    for b, half in enumerate(tiles(s % NQ)):
                        for j, (c, _) in enumerate(half):
                            mm = nc.tensor.transpose(T[b][:, j, :], sb[:, s % 2, c:c + P], K.ident[:])
                    mm.then_inc(t_done, 1)

                def weigh_values(i, s):
                    h2, t = divmod(s, NQ)
                    pe.wait_ge(tv_out, i * NS + (s + 1))
                    pe.wait_ge(ta_out, i * NS + (s + 1))
                    pe.wait_ge(o_out, i * NS + s)
                    seen = [(b * 4 + j, vt) for b, half in enumerate(tiles(t)) for j, (_, vt) in enumerate(half)]
                    for n, (j, vt) in enumerate(seen):
                        mm = nc.tensor.matmul(O[s % 2][:, 0:HD], aT[:, j, :], v[:, vt, h2 * HD:(h2 + 1) * HD],
                                              start=(n == 0), stop=(n == len(seen) - 1))
                    mm.then_inc(o_done, 1)

                with pe.Fori(0, TURNS) as i:
                    if near:
                        pe.wait_ge(q_in, i * 16 + 16)
                        pe.wait_ge(k_in, i * 16 + 16)
                    else:
                        pe.wait_ge(ready, i + 2)
                    pe.wait_ge(b_done, i * NS)
                    pe.wait_ge(tv_out, i * NS)
                    pe.wait_ge(ta_out, i * NS)
                    for m, (src, raw) in enumerate(((q, q), (k, k)) if near else ((qr, q), (kr, k))):
                        for t in range(NT):
                            to = S[m][:, t * P:(t + 1) * P] if t < 8 else T[m][:, t - 8, :]
                            mm = nc.tensor.transpose(to, (src if t < NTX else raw)[:, t, :], K.ident[:])
                    mm.then_inc(prep_done, 1)
                    pe.wait_ge(qt_done, i + 1)
                    pe.wait_ge(kt_done, i + 1)
                    score(i, 0)
                    for s in range(NS):
                        if s + 1 < NS:
                            score(i, s + 1)
                        turn_weights(i, s)
                        if s == 0:
                            pe.wait_ge(v_in, i * 16 + 16)
                        weigh_values(i, s)



def row(vec, width):
    return vec.rearrange("(a n) -> a n", a=1).broadcast_to([P, width])


def pipelined(eng, tiles, link, per, main, tail):
    cond = 1 if tiles == NT else 0
    main(0, 0)
    with eng.Fori(0, (tiles - 2) // 2) as i:
        link.turn(i, 2 * per)
        main(i * 2 + 1, 1)
        tail(i * 2, 0, 0)
        main(i * 2 + 2, 0)
        tail(i * 2 + 1, 1, 0)
    link.over((tiles - 2) // 2)
    main(tiles - 1, 1)
    tail(tiles - 2, 0, cond)
    tail(tiles - 1, 1, cond)


def mix_out(nc, name, K, tiles, mixed, w_out, mod, g_post, g_pre, w_router, res, normed, affinity):
    with Stage(nc, name) as st:
        w = st.sb("w", [P, KD, D])
        wr = st.sb("wr", [P, KD, E])
        ot = st.sb("ot", [P, 2, D])
        oT = st.sb("oT", [P, KD, P])
        xr = st.sb("xr", [P, 2, D])
        tmp = st.sb("tmp", [P, D])
        xn = st.sb("xn", [P, 2, D])
        hT = st.sb("hT", [P, KD, P])
        sq = st.sb("sq", [P, D])
        gpost = st.sb("gpost", [P, D])
        gate = st.sb("gate", [P, 2, D])
        g = st.sb("g", [P, KD])
        shift = st.sb("shift", [P, 2, KD])
        gain = st.sb("gain", [P, 2, KD])
        ms = st.sb("ms", [P, 2, 2])
        rs = st.sb("rs", [P, 2, 2])
        nmx = st.sb("nmx", [P, 1])
        ex = st.sb("ex", [P, E])
        es = st.sb("es", [P, 1])
        af = st.sb("af", [E, 2, P])
        TP = [st.ps(f"tp{h}", [P, 4, P]) for h in range(2)]
        Y = [st.ps(f"y{s}", [P, 2, BANK]) for s in range(2)]
        L = st.ps("l", [P, BANK])
        A = st.ps("a", [P, BANK])
        (w_in, vec_in, vec_done, to_done, otv, ota, y_done, ms1, rs1, r_done, x_done, ms2, rs2, xn_done, tx_done, hv, ha,
         l_done, mx_done, ex_done, aff_done, at_done, af_done, act_step, dve_step, pool_step) = (st.sem(n) for n in (
             "w_in vec_in vec_done to_done otv ota y_done ms1 rs1 r_done x_done ms2 rs2 xn_done tx_done hv ha "
             "l_done mx_done ex_done aff_done at_done af_done act_step dve_step pool_step").split())
        o_in, x_in, x_out, n_out, a_out = ([st.sem(f"{n}{s}") for s in range(2)] for n in ("o_in", "x_in", "x_out", "n_out", "a_out"))
        begun = st.sem("begun")
        conds = 2 if tiles == NT else 1

        with nc.Block() as block:

            @block.sync
            def _(sp):
                for c in range(conds):
                    sp.dma_start(gate[:, c, :], row(mod[c, 2 * D:3 * D], D)).then_inc(vec_in, 16)
                    sp.dma_start(shift[:, c, :], columns(mod[c, 3 * D:4 * D])).then_inc(vec_in, 16)
                    sp.dma_start(gain[:, c, :], columns(mod[c, 4 * D:5 * D])).then_inc(vec_in, 16)
                sp.dma_start(gpost[:], row(g_post, D)).then_inc(vec_in, 16)
                sp.dma_start(g[:], columns(g_pre)).then_inc(vec_in, 16)

                def load(n, slot, half):
                    before, at = n - 1, bass.ds(n * P, P)
                    after(sp, to_done, before)
                    sp.dma_start(ot[:, slot, :], mixed[at, :]).then_inc(o_in[slot], 16)
                    after(sp, xn_done, before)
                    sp.sem_inc(begun, 1)
                    after(sp, x_out[slot], half * 16)
                    sp.dma_start(xr[:, slot, :], res[at, :]).then_inc(x_in[slot], 16)

                load(0, 0, 0)
                sp.dma_start(w[:], w_out.rearrange("(k p) n -> p k n", p=P)).then_inc(w_in, 16)
                sp.dma_start(wr[:], w_router.rearrange("(k p) n -> p k n", p=P)).then_inc(w_in, 16)
                load(1, 1, 0)
                with sp.Fori(1, tiles // 2) as i:
                    for slot in range(2):
                        load(i * 2 + slot, slot, i)

            @block.gpsimd
            def _(pool):
                link = Link(pool, pool_step)

                def rsqrt(n, slot, which, done):
                    at = ms[:, slot, which:which + 1]
                    link(nc.gpsimd.tensor_tensor(at, at, K.eps[:, 0:1], ALU.add))
                    nc.gpsimd.tensor_tensor(rs[:, slot, which:which + 1], at, K.neg_half[:, 0:1], ALU.pow).then_inc(done, 1)

                def tail(n, slot, cond):
                    pool.wait_ge(ms1, n + 1)
                    rsqrt(n, slot, 0, rs1)
                    pool.wait_ge(r_done, n + 1)
                    pool.wait_ge(x_in[slot], n * 8 + 16 - slot * 8)
                    nc.gpsimd.tensor_tensor(xr[:, slot, :], tmp[:], xr[:, slot, :], ALU.add).then_inc(x_done, 1)
                    pool.wait_ge(ms2, n + 1)
                    rsqrt(n, slot, 1, rs2)

                pipelined(pool, tiles, link, 2, lambda n, slot: None, tail)

            @block.scalar
            def _(act):
                link = Link(act, act_step)

                def main(n, slot):
                    act.wait_ge(to_done, n + 1)
                    nc.scalar.activation(oT[:, 4:8, :], TP[1][:], ACT.Copy).then_inc(ota, 1)

                def tail(n, slot, cond):
                    act.wait_ge(y_done, n + 1)
                    nc.scalar.activation(sq[:], Y[slot][:].rearrange("p a b -> p (a b)"), ACT.Square, scale=D ** -0.5,
                                         accum_out=ms[:, slot, 0:1]).then_inc(ms1, 1)
                    act.wait_ge(x_done, n + 1)
                    nc.scalar.activation(sq[:], xr[:, slot, :], ACT.Square, scale=D ** -0.5,
                                         accum_out=ms[:, slot, 1:2]).then_inc(ms2, 1)
                    act.wait_ge(rs2, n + 1)
                    after(act, n_out[slot], n * 8 - slot * 8)
                    nc.scalar.activation(xn[:, slot, :], xr[:, slot, :], ACT.Copy, scale=rs[:, slot, 1:2]).then_inc(xn_done, 1)
                    act.wait_ge(xn_done, n + 1)
                    at = n * P if isinstance(n, int) else act.snap(n * P)
                    act.dma_start(res[bass.ds(at, P), :], xr[:, slot, :]).then_inc(x_out[slot], 16)
                    act.dma_start(normed[bass.ds(at, P), :], xn[:, slot, :]).then_inc(n_out[slot], 16)
                    act.wait_ge(tx_done, n + 1)
                    for k in range(4, KD):
                        a = nc.scalar.activation(hT[:, k, :], TP[1][:, k - 4, :], ACT.Identity, bias=shift[:, cond, k:k + 1],
                                                 scale=gain[:, cond, k:k + 1])
                    a.then_inc(ha, 1)
                    act.wait_ge(mx_done, n + 1)
                    nc.scalar.activation(ex[:], L[:, 0:E], ACT.Exp, bias=nmx[:], accum_out=es[:]).then_inc(ex_done, 1)
                    act.wait_ge(af_done, n + 1)
                    at = n * P if isinstance(n, int) else act.snap(n * P)
                    act.dma_start(affinity[:, bass.ds(at, P)], af[:, slot, :]).then_inc(a_out[slot], 16)

                act.wait_ge(vec_done, conds * 2)
                pipelined(act, tiles, link, 0, main, tail)
                for slot in range(2):
                    for out in (x_out, n_out, a_out):
                        act.wait_ge(out[slot], 16 * tiles // 2)

            @block.vector
            def _(dve):
                link = Link(dve, dve_step)
                dve.wait_ge(vec_in, 16 * (3 * conds + 2))
                for c in range(conds):
                    nc.vector.scalar_tensor_tensor(gain[:, c, :], gain[:, c, :], 1.0, g[:], ALU.add, ALU.mult).then_inc(vec_done, 1)
                    nc.vector.tensor_tensor(gate[:, c, :], gate[:, c, :], gpost[:], ALU.mult).then_inc(vec_done, 1)
                dve.wait_ge(vec_done, conds * 2)

                def main(n, slot):
                    dve.wait_ge(to_done, n + 1)
                    nc.vector.tensor_copy(oT[:, 0:4, :], TP[0][:]).then_inc(otv, 1)

                def tail(n, slot, cond):
                    dve.wait_ge(rs1, n + 1)
                    nc.vector.scalar_tensor_tensor(tmp[:], Y[slot][:].rearrange("p a b -> p (a b)"), rs[:, slot, 0:1], gate[:, cond, :],
                                                   ALU.mult, ALU.mult).then_inc(r_done, 1)
                    dve.wait_ge(tx_done, n + 1)
                    for k in range(4):
                        v = nc.vector.tensor_scalar(hT[:, k, :], TP[0][:, k, :], gain[:, cond, k:k + 1], shift[:, cond, k:k + 1],
                                                    ALU.mult, ALU.add)
                    v.then_inc(hv, 1)
                    dve.wait_ge(l_done, n + 1)
                    nc.vector.tensor_reduce(nmx[:], L[:, 0:E], AX.X, ALU.max, negate=True).then_inc(mx_done, 1)
                    dve.wait_ge(ex_done, n + 1)
                    link(nc.vector.reciprocal(es[:], es[:]))
                    nc.vector.tensor_scalar(ex[:], ex[:], es[:], None, ALU.mult).then_inc(aff_done, 1)
                    dve.wait_ge(at_done, n + 1)
                    after(dve, a_out[slot], n * 8 - slot * 8)
                    nc.vector.tensor_copy(af[:, slot, :], A[0:E, 0:P]).then_inc(af_done, 1)

                pipelined(dve, tiles, link, 1, main, tail)

            @block.tensor
            def _(pe):
                def main(n, slot):
                    pe.wait_ge(o_in[slot], n * 8 + 16 - slot * 8)
                    after(pe, hv, n - 1)
                    after(pe, ha, n - 1)
                    for k in range(KD):
                        mm = nc.tensor.transpose(TP[k // 4][:, k % 4, :], ot[:, slot, k * P:(k + 1) * P], K.ident[:])
                    mm.then_inc(to_done, 1)
                    after(pe, r_done, n - 1)
                    pe.wait_ge(otv, n + 1)
                    pe.wait_ge(ota, n + 1)
                    for half in range(2):
                        for k in range(KD):
                            mm = nc.tensor.matmul(Y[slot][:, half, :], oT[:, k, :], w[:, k, half * BANK:(half + 1) * BANK],
                                                  start=(k == 0), stop=(k == KD - 1))
                    mm.then_inc(y_done, 1)

                def tail(n, slot, cond):
                    pe.wait_ge(xn_done, n + 1)
                    for k in range(KD):
                        mm = nc.tensor.transpose(TP[k // 4][:, k % 4, :], xn[:, slot, k * P:(k + 1) * P], K.ident[:])
                    mm.then_inc(tx_done, 1)
                    pe.wait_ge(hv, n + 1)
                    pe.wait_ge(ha, n + 1)
                    for k in range(KD):
                        mm = nc.tensor.matmul(L[:, 0:E], hT[:, k, :], wr[:, k, :], start=(k == 0), stop=(k == KD - 1))
                    mm.then_inc(l_done, 1)
                    pe.wait_ge(aff_done, n + 1)
                    nc.tensor.transpose(A[0:E, 0:P], ex[:], K.ident[:]).then_inc(at_done, 1)

                pe.wait_ge(w_in, 32)
                pipelined(pe, tiles, Link(pe, None), 0, main, tail)


def choose(nc, name, with_ctx, affinity, index, weight, index_c, weight_c):
    with Stage(nc, name) as st:
        work = st.sb("work", [E, ROWS])
        val = st.sb("val", [E, CAPX + CAPC])
        idx = st.sb("idx", [E, CAPX + CAPC], U32)
        idf = st.sb("idf", [E, CAPC])
        a_in, step, stored = (st.sem(n) for n in ("a_in", "step", "stored"))
        parts = [(0, SEQ, 0, CAPX, index, weight)] + ([(SEQ, CTX, CAPX, CAPC, index_c, weight_c)] if with_ctx else [])
        n_cols = ROWS if with_ctx else SEQ
        steps = sum(cap // 8 * 3 for *_, cap, _, _ in parts) + (2 if with_ctx else 0)

        with nc.Block() as block:

            @block.sync
            def _(sp):
                sp.dma_start(work[:, 0:n_cols], affinity[:, 0:n_cols]).then_inc(a_in, 16)
                sp.wait_ge(step, steps)
                for _, _, to, cap, ix, wt in parts:
                    sp.dma_start(ix[0:E, :], idx[:, to:to + cap].bitcast(I32)).then_inc(stored, 16)
                    sp.dma_start(ix[E:E + 1, :], idx[0:1, to:to + cap].bitcast(I32)).then_inc(stored, 16)
                    sp.dma_start(wt, val[:, to:to + cap]).then_inc(stored, 16)
                sp.wait_ge(stored, 48 * len(parts))

            @block.vector
            def _(dve):
                link = Link(dve, step)
                dve.wait_ge(a_in, 16)
                for first, n, to, cap, _, _ in parts:
                    left = work[:, first:first + n]
                    for j in range(to, to + cap, 8):
                        link(nc.vector.max(val[:, j:j + 8], left))
                        link(nc.vector.max_index(idx[:, j:j + 8], val[:, j:j + 8], left))
                        link(nc.vector.match_replace(left, val[:, j:j + 8], left, -1.0))
                if with_ctx:
                    link(nc.vector.tensor_copy(idf[:], idx[:, CAPX:CAPX + CAPC]))
                    link(nc.vector.tensor_scalar(idx[:, CAPX:CAPX + CAPC], idf[:], float(SEQ), None, ALU.add))
                assert link.n == steps


def experts(nc, name, K, with_ctx, normed, mod, g_pre, index, weight, index_c, weight_c, w_gate, w_up, w_down, moe):
    N = CAPX + (CAPC if with_ctx else 0)
    HALF = 4
    rows_out = ROWS if with_ctx else SEQ
    with Stage(nc, name) as st:
        wg = st.sb("wg", [P, 2, KD, BANK])
        wu = st.sb("wu", [P, 2, KD, BANK])
        wd = st.sb("wd", [P, 2, KD, BANK])
        xg = st.sb("xg", [P, D])
        xT = st.sb("xT", [P, KD, N])
        hid = st.sb("hid", [P, KD, N])
        sil = st.sb("sil", [P, 2, N])
        y = st.sb("y", [P, D])
        ixg = st.sb("ixg", [P, 1], I32)
        ixs = st.sb("ixs", [P, 1], I32)
        wt = st.sb("wt", [P, 1])
        g = st.sb("g", [P, KD])
        shift = st.sb("shift", [P, 2, KD])
        gain = st.sb("gain", [P, 2, KD])
        GU = [st.ps(f"gu{s}", [P, 2, 256]) for s in range(2)]
        TP = [st.ps(f"tp{h}", [P, 4, P]) for h in range(2)]
        Y = [st.ps(f"y{h}", [P, BANK]) for h in range(2)]
        conds = 2 if with_ctx else 1
        if with_ctx:
            xc = st.sb("xc", [CAPC, D])
            yc = st.sb("yc", [CAPC, D])
            ixgc = st.sb("ixgc", [CAPC, 1], I32)
            ixsc = st.sb("ixsc", [CAPC, 1], I32)
            wtc = st.sb("wtc", [CAPC, 1])
            TC = st.ps("tc", [P, KD, CAPC])
            YC = st.ps("yc", [CAPC, BANK])
        (vec_in, vec_done, zeroed, zeros_in, ixg_in, ixs_in, tp_done, xv, xa, xcd, gu_done, sil_done, hid_done,
         y_done, yv, ya, yc_done, yc_out, act_step, dve_step) = (st.sem(n) for n in (
             "vec_in vec_done zeroed zeros_in ixg_in ixs_in tp_done xv xa xcd gu_done sil_done hid_done "
             "y_done yv ya yc_done yc_out act_step dve_step").split())
        begun = st.sem("begun")
        g_done, s_done = st.pool_sem(K, "g_done"), st.pool_sem(K, "s_done")
        w_in = {n: [st.sem(f"{n}_in{h}") for h in range(2)] for n in ("wg", "wu", "wd")}
        IX = 32 if with_ctx else 16
        IS = 64 if with_ctx else 32

        def half_of(weights, e, h):
            return weights[bass.ds(e, 1), :, h * BANK:(h + 1) * BANK].rearrange("a (k p) n -> p (a k) n", p=P)

        def column(table, e):
            return table[bass.ds(e, 1), :].rearrange("a p -> p a")

        with nc.Block() as block:

            @block.sync
            def _(sp):
                sp.dma_start(ixg[:], column(index, 0)).then_inc(ixg_in, 16)
                if with_ctx:
                    sp.dma_start(ixgc[:], column(index_c, 0)).then_inc(ixg_in, 16)
                for c in range(conds):
                    sp.dma_start(shift[:, c, :], columns(mod[c, 3 * D:4 * D])).then_inc(vec_in, 16)
                    sp.dma_start(gain[:, c, :], columns(mod[c, 4 * D:5 * D])).then_inc(vec_in, 16)
                sp.dma_start(g[:], columns(g_pre)).then_inc(vec_in, 16)
                sp.wait_ge(zeroed, 1)
                for t in range(rows_out // P):
                    sp.dma_start(moe[t * P:(t + 1) * P, :], y[:]).then_inc(zeros_in, 16)
                with sp.Fori(0, E) as e:
                    for h in range(2):
                        sp.wait_ge(gu_done, e * 8 + HALF * (h + 1))
                        sp.dma_start(wg[:, h], half_of(w_gate, e, h)).then_inc(w_in["wg"][h], 16)
                        sp.dma_start(wu[:, h], half_of(w_up, e, h)).then_inc(w_in["wu"][h], 16)
                    for h in range(2):
                        sp.wait_ge(y_done, e * 2 + (h + 1))
                        sp.dma_start(wd[:, h], half_of(w_down, e, h)).then_inc(w_in["wd"][h], 16)
                    sp.wait_ge(s_done, e * IX)
                    sp.dma_start(ixs[:], column(index, e)).then_inc(ixs_in, 16)
                    sp.dma_start(wt[:], column(weight, e)).then_inc(ixs_in, 16)
                    if with_ctx:
                        sp.dma_start(ixsc[:], column(index_c, e)).then_inc(ixs_in, 16)
                        sp.dma_start(wtc[:], column(weight_c, e)).then_inc(ixs_in, 16)
                    sp.wait_ge(g_done, e * IX + IX)
                    sp.dma_start(ixg[:], column(index, e + 1)).then_inc(ixg_in, 16)
                    if with_ctx:
                        sp.dma_start(ixgc[:], column(index_c, e + 1)).then_inc(ixg_in, 16)

            @block.gpsimd
            def _(pool):
                def gather(e):
                    pool.wait_ge(ixg_in, e * IX + IX)
                    after(pool, tp_done, e)
                    pool.sem_inc(begun, 1)
                    pool.indirect_dma_start(xg[:], None, normed, bass.IndirectOffsetOnAxis(ap=ixg[:, 0:1], axis=0)).then_inc(g_done, 16)
                    if with_ctx:
                        pool.indirect_dma_start(xc[:], None, normed, bass.IndirectOffsetOnAxis(ap=ixgc[:, 0:1], axis=0)).then_inc(g_done, 16)

                pool.wait_ge(vec_done, 1)
                nc.gpsimd.memset(y[:], 0.0).then_inc(zeroed, 1)
                gather(0)
                pool.wait_ge(zeros_in, 16 * (rows_out // P))
                with pool.Fori(0, E) as e:
                    gather(e + 1)
                    pool.wait_ge(ixs_in, e * IS + IS)
                    pool.wait_ge(yv, e + 1)
                    pool.wait_ge(ya, e + 1)
                    if with_ctx:
                        pool.wait_ge(yc_out, e * 2 + 2)
                    pool.wait_ge(s_done, e * IX)
                    pool.sem_inc(begun, 1)
                    pool.indirect_dma_start(moe, bass.IndirectOffsetOnAxis(ap=ixs[:, 0:1], axis=0), y[:], None,
                                            compute_op=ALU.add).then_inc(s_done, 16)
                    if with_ctx:
                        pool.indirect_dma_start(moe, bass.IndirectOffsetOnAxis(ap=ixsc[:, 0:1], axis=0), yc[:], None,
                                                compute_op=ALU.add).then_inc(s_done, 16)
                pool.wait_ge(s_done, E * IX)
                pool.wait_ge(g_done, (E + 1) * IX)

            @block.scalar
            def _(act):
                link = Link(act, act_step)

                def transposed(e):
                    act.wait_ge(tp_done, e + 1)
                    for k in range(4, KD):
                        a = nc.scalar.activation(xT[:, k, 0:CAPX], TP[1][:, k - 4, :], ACT.Identity, bias=shift[:, 0, k:k + 1],
                                                 scale=gain[:, 0, k:k + 1])
                    a.then_inc(xa, 1)

                act.wait_ge(vec_done, conds)
                transposed(0)
                with act.Fori(0, E) as e:
                    for f in range(KD):
                        act.wait_ge(gu_done, e * KD + (f + 1 + KD))
                        if f >= 2:
                            act.wait_ge(hid_done, e * KD + (f - 1))
                        nc.scalar.activation(sil[:, f % 2, :], GU[f % 2][:, 0, 0:N], ACT.Silu).then_inc(sil_done, 1)
                    transposed(e + 1)
                    act.wait_ge(ixs_in, e * IS + IS)
                    act.wait_ge(y_done, e * 2 + 3)
                    nc.scalar.activation(y[:, 0:BANK], Y[0][:], ACT.Copy, scale=wt[:]).then_inc(ya, 1)
                    if with_ctx:
                        for h in range(2):
                            act.wait_ge(yc_done, e * 2 + (h + 1))
                            nc.scalar.activation(yc[:, h * BANK:(h + 1) * BANK], YC[:], ACT.Copy, scale=wtc[:]).then_inc(yc_out, 1)

            @block.vector
            def _(dve):
                link = Link(dve, dve_step)

                def transposed(e):
                    dve.wait_ge(tp_done, e + 1)
                    for k in range(4):
                        v = nc.vector.tensor_scalar(xT[:, k, 0:CAPX], TP[0][:, k, :], gain[:, 0, k:k + 1], shift[:, 0, k:k + 1],
                                                    ALU.mult, ALU.add)
                    v.then_inc(xv, 1)
                    if with_ctx:
                        to = xT[:, :, CAPX:N]
                        link(nc.vector.tensor_tensor(to, TC[:], gain[:, 1, :].unsqueeze(2).to_broadcast([P, KD, CAPC]), ALU.mult))
                        nc.vector.tensor_tensor(to, to, shift[:, 1, :].unsqueeze(2).to_broadcast([P, KD, CAPC]), ALU.add).then_inc(xcd, 1)

                dve.wait_ge(vec_in, 16 * (2 * conds + 1))
                for c in range(conds):
                    nc.vector.scalar_tensor_tensor(gain[:, c, :], gain[:, c, :], 1.0, g[:], ALU.add, ALU.mult).then_inc(vec_done, 1)
                dve.wait_ge(vec_done, conds)
                transposed(0)
                with dve.Fori(0, E) as e:
                    link.turn(e, 1 if with_ctx else 0)
                    for f in range(KD):
                        dve.wait_ge(sil_done, e * KD + (f + 1))
                        nc.vector.tensor_tensor(hid[:, f, :], sil[:, f % 2, :], GU[f % 2][:, 1, 0:N], ALU.mult).then_inc(hid_done, 1)
                    transposed(e + 1)
                    dve.wait_ge(ixs_in, e * IS + IS)
                    dve.wait_ge(y_done, e * 2 + 4)
                    nc.vector.tensor_scalar(y[:, BANK:D], Y[1][:], wt[:], None, ALU.mult).then_inc(yv, 1)
                link.over(E)

            @block.tensor
            def _(pe):
                pe.sem_inc(gu_done, KD)
                pe.sem_inc(y_done, 2)

                def turn_rows(e):
                    pe.wait_ge(g_done, e * IX + IX)
                    for k in range(KD):
                        mm = nc.tensor.transpose(TP[k // 4][:, k % 4, :], xg[:, k * P:(k + 1) * P], K.ident[:])
                    if with_ctx:
                        for k in range(KD):
                            mm = nc.tensor.transpose(TC[:, k, :], xc[:, k * P:(k + 1) * P], K.ident[0:CAPC, 0:CAPC])
                    mm.then_inc(tp_done, 1)

                turn_rows(0)
                with pe.Fori(0, E) as e:
                    pe.wait_ge(xv, e + 1)
                    pe.wait_ge(xa, e + 1)
                    if with_ctx:
                        pe.wait_ge(xcd, e + 1)
                    for f in range(KD):
                        h, c = divmod(f, HALF)
                        if c == 0:
                            pe.wait_ge(w_in["wg"][h], e * 16 + 16)
                            pe.wait_ge(w_in["wu"][h], e * 16 + 16)
                        if f >= 2:
                            pe.wait_ge(hid_done, e * KD + (f - 1))
                        for part, w in enumerate((wg, wu)):
                            for k in range(KD):
                                mm = nc.tensor.matmul(GU[f % 2][:, part, 0:N], w[:, h, k, c * P:(c + 1) * P], xT[:, k, :],
                                                      start=(k == 0), stop=(k == KD - 1))
                        mm.then_inc(gu_done, 1)
                    turn_rows(e + 1)
                    pe.wait_ge(hid_done, e * KD + KD)
                    for h in range(2):
                        pe.wait_ge(w_in["wd"][h], e * 16 + 16)
                        pe.wait_ge((ya, yv)[h], e)
                        if with_ctx:
                            pe.wait_ge(yc_out, e * 2 + h)
                            for k in range(KD):
                                mm = nc.tensor.matmul(YC[:], hid[:, k, CAPX:N], wd[:, h, k, :], start=(k == 0), stop=(k == KD - 1))
                            mm.then_inc(yc_done, 1)
                        for k in range(KD):
                            mm = nc.tensor.matmul(Y[h][:], hid[:, k, 0:CAPX], wd[:, h, k, :], start=(k == 0), stop=(k == KD - 1))
                        mm.then_inc(y_done, 1)


def finish(nc, name, K, tiles, moe, mod, g_post, res, out):
    conds = 2 if tiles == NT else 1
    with Stage(nc, name) as st:
        m = st.sb("m", [P, 2, D])
        x = st.sb("x", [P, 2, D])
        sq = st.sb("sq", [P, D])
        ms = st.sb("ms", [P, 2])
        rs = st.sb("rs", [P, 2])
        gpost = st.sb("gpost", [P, D])
        gate = st.sb("gate", [P, 2, D])
        vec_in, vec_done, ms_done, rs_done, m_done, x_done, act_step, pool_step = (st.sem(n) for n in (
            "vec_in vec_done ms_done rs_done m_done x_done act_step pool_step").split())
        m_in, x_in, stored = ([st.sem(f"{n}{s}") for s in range(2)] for n in ("m_in", "x_in", "stored"))

        def over_tiles(eng, step, link=None, per=0):
            with eng.Fori(0, NTX // 2) as i:
                if link:
                    link.turn(i, per)
                for s in range(2):
                    step(i, s, 0)
            if link:
                link.over(NTX // 2)
            for s in range(2) if conds == 2 else ():
                step(NTX // 2, s, 1)

        with nc.Block() as block:

            @block.sync
            def _(sp):
                for c in range(conds):
                    sp.dma_start(gate[:, c, :], row(mod[c, 5 * D:6 * D], D)).then_inc(vec_in, 16)
                sp.dma_start(gpost[:], row(g_post, D)).then_inc(vec_in, 16)

                def load(i, s, cond):
                    at = bass.ds(i * (2 * P) + s * P, P)
                    after(sp, stored[s], i * 16)
                    sp.dma_start(m[:, s, :], moe[at, :]).then_inc(m_in[s], 16)
                    sp.dma_start(x[:, s, :], res[at, :]).then_inc(x_in[s], 16)
                over_tiles(sp, load)

            @block.scalar
            def _(act):
                def step(i, s, cond):
                    act.wait_ge(m_in[s], i * 16 + 16)
                    nc.scalar.activation(sq[:], m[:, s, :], ACT.Square, scale=D ** -0.5, accum_out=ms[:, s:s + 1]).then_inc(ms_done, 1)
                    act.wait_ge(ms_done, i * 2 + (s + 1))

                def store(i, s, cond):
                    act.wait_ge(x_done, i * 2 + (s + 1))
                    at = i * (2 * P) + s * P
                    at = at if isinstance(at, int) else act.snap(at)
                    act.dma_start(out[bass.ds(at, P), :], x[:, s, :]).then_inc(stored[s], 16)

                def both(i, s, cond):
                    step(i, s, cond)
                    if s == 1:
                        store(i, 0, cond)
                        store(i, 1, cond)
                over_tiles(act, both)
                for s in range(2):
                    act.wait_ge(stored[s], 16 * tiles // 2)

            @block.gpsimd
            def _(pool):
                link = Link(pool, pool_step)

                def step(i, s, cond):
                    at = ms[:, s:s + 1]
                    pool.wait_ge(ms_done, i * 2 + (s + 1))
                    link(nc.gpsimd.tensor_tensor(at, at, K.eps[:, 0:1], ALU.add))
                    nc.gpsimd.tensor_tensor(rs[:, s:s + 1], at, K.neg_half[:, 0:1], ALU.pow).then_inc(rs_done, 1)
                    pool.wait_ge(m_done, i * 2 + (s + 1))
                    pool.wait_ge(x_in[s], i * 16 + 16)
                    nc.gpsimd.tensor_tensor(x[:, s, :], m[:, s, :], x[:, s, :], ALU.add).then_inc(x_done, 1)
                over_tiles(pool, step, link, 2)

            @block.vector
            def _(dve):
                dve.wait_ge(vec_in, 16 * (conds + 1))
                for c in range(conds):
                    nc.vector.tensor_tensor(gate[:, c, :], gate[:, c, :], gpost[:], ALU.mult).then_inc(vec_done, 1)
                dve.wait_ge(vec_done, conds)

                def step(i, s, cond):
                    dve.wait_ge(rs_done, i * 2 + (s + 1))
                    nc.vector.scalar_tensor_tensor(m[:, s, :], m[:, s, :], rs[:, s:s + 1], gate[:, cond, :], ALU.mult, ALU.mult).then_inc(m_done, 1)
                over_tiles(dve, step)


SCAN_TILES = NTC + NTX + NTC
SCAN_ROWS = SCAN_TILES * P
HEADS_D, GROUPS_D = 8, 2
INNER = HEADS_D * HD
XBC0, Z0, DT0 = 768, 1792, 2304


def convolve(nc, K, proj, conv_w, conv_b, by_channel, by_token):
    TAPS, PAD = 5, 2
    XLEN, CLEN = SEQ + 2 * PAD, CTX + 2 * PAD
    N = XLEN + CLEN - 2 * PAD
    XS, CS = slice(0, SEQ), slice(XLEN, XLEN + CTX)
    with Stage(nc, "conv") as st:
        xin = st.sb("xin", [P, NT, P])
        pad = st.sb("pad", [P, XLEN + CLEN])
        acc = st.sb("acc", [P, N])
        u = st.sb("u", [P, N])
        ut = st.sb("ut", [P, NT, P])
        cw = st.sb("cw", [P, TAPS + 1, KD])
        cur = st.sb("cur", [P, TAPS + 1])
        T = [st.ps(f"t{s}", [P, 3 * BANK]) for s in range(2)]
        (cw_in, x_in, padded, tx_done, pad_done, cur_done, acc_done, u_done, tu_done, ut_done, u_out, ut_out, dve_step) = (
            st.sem(n) for n in "cw_in x_in padded tx_done pad_done cur_done acc_done u_done tu_done ut_done u_out ut_out dve_step".split())

        with nc.Block() as block:

            @block.sync
            def _(sp):
                for d in range(TAPS):
                    sp.dma_start(cw[:, d, :], columns(conv_w[d, 0])).then_inc(cw_in, 16)
                sp.dma_start(cw[:, TAPS, :], columns(conv_b)).then_inc(cw_in, 16)
                with sp.Fori(0, KD) as i:
                    sp.wait_ge(tx_done, i)
                    sp.dma_start(xin[:], proj.rearrange("(t p) n -> p t n", p=P)[:, :, bass.ds(i * P + XBC0, P)]).then_inc(x_in, 16)

            @block.gpsimd
            def _(pool):
                nc.gpsimd.memset(pad[:], 0.0).then_inc(padded, 1)

            @block.scalar
            def _(act):
                act.wait_ge(padded, 1)
                with act.Fori(0, KD) as i:
                    act.wait_ge(tx_done, i + 1)
                    act.wait_ge(acc_done, i)
                    nc.scalar.activation(pad[:, PAD:PAD + SEQ], T[0][:, 0:SEQ], ACT.Copy).then_inc(pad_done, 1)
                    nc.scalar.activation(pad[:, XLEN + PAD:XLEN + PAD + CTX], T[0][:, SEQ:ROWS], ACT.Copy).then_inc(pad_done, 1)
                    act.wait_ge(acc_done, i + 1)
                    act.wait_ge(tu_done, i)
                    act.wait_ge(u_out, i * 48)
                    nc.scalar.activation(u[:], acc[:], ACT.Silu, bias=cur[:, TAPS:TAPS + 1]).then_inc(u_done, 1)
                    act.wait_ge(u_done, i + 1)
                    at = act.snap(i * P)
                    for to, part in ((0, CS), (CTX, XS), (CTX + SEQ, CS)):
                        act.dma_start(by_channel[bass.ds(at, P), to:to + part.stop - part.start], u[:, part]).then_inc(u_out, 16)
                    act.wait_ge(ut_done, i + 1)
                    at = act.snap(i * P)
                    rows = by_token.rearrange("(t p) n -> p t n", p=P)
                    for to, first, n in ((0, NTX, NTC), (NTC, 0, NTX), (NTC + NTX, NTX, NTC)):
                        act.dma_start(rows[:, to:to + n, bass.ds(at, P)], ut[:, first:first + n, :]).then_inc(ut_out, 16)
                act.wait_ge(u_out, KD * 48)
                act.wait_ge(ut_out, KD * 48)

            @block.vector
            def _(dve):
                link = Link(dve, dve_step)
                dve.wait_ge(cw_in, 16 * (TAPS + 1))
                with dve.Fori(0, KD) as i:
                    link.turn(i, TAPS)
                    dve.wait_ge(u_done, i)
                    link(nc.vector.tensor_copy(cur[:], cw[:, :, bass.ds(i, 1)].rearrange("p d k -> p (d k)")))
                    dve.wait_ge(pad_done, i * 2 + 2)
                    link(nc.vector.tensor_scalar(acc[:], pad[:, 0:N], cur[:, 0:1], None, ALU.mult))
                    for d in range(1, TAPS):
                        c = nc.vector.scalar_tensor_tensor(acc[:], pad[:, d:d + N], cur[:, d:d + 1], acc[:], ALU.mult, ALU.add)
                        if d < TAPS - 1:
                            link(c)
                    c.then_inc(acc_done, 1)
                    dve.wait_ge(tu_done, i + 1)
                    dve.wait_ge(ut_out, i * 48)
                    nc.vector.tensor_copy(ut[:].rearrange("p t n -> p (t n)"), T[1][:, 0:ROWS]).then_inc(ut_done, 1)
                link.over(KD)

            @block.tensor
            def _(pe):
                with pe.Fori(0, KD) as i:
                    pe.wait_ge(x_in, i * 16 + 16)
                    pe.wait_ge(pad_done, i * 2)
                    for t in range(NT):
                        mm = nc.tensor.transpose(T[0][:, t * P:(t + 1) * P], xin[:, t, :], K.ident[:])
                    mm.then_inc(tx_done, 1)
                    pe.wait_ge(u_done, i + 1)
                    pe.wait_ge(ut_done, i)
                    for t in range(NT):
                        c = t * P if t < NTX else XLEN + (t - NTX) * P
                        mm = nc.tensor.transpose(T[1][:, t * P:(t + 1) * P], u[:, c:c + P], K.ident[:])
                    mm.then_inc(tu_done, 1)


def scan(nc, K, proj, by_channel, by_token, a_logs, dt_biases, y_out):
    TURNS = NTC + NTX
    H8 = HEADS_D
    with Stage(nc, "scan") as st:
        dt = st.sb("dt", [P, SCAN_TILES, 2 * H8])
        da = st.sb("da", [P, SCAN_TILES, 2 * H8])
        sp_a = st.sb("sp_a", [P, SCAN_TILES, 2 * H8])
        sp_b = st.sb("sp_b", [P, SCAN_TILES, 2 * H8])
        alog = st.sb("alog", [P, 2 * H8])
        dtb = st.sb("dtb", [P, 2 * H8])
        tri = st.sb("tri", [P, 2, P])
        bc = st.sb("bc", [P, 2, 2 * GROUPS_D, P])
        xb = st.sb("xb", [P, 2, INNER + GROUPS_D * P])
        dtc = st.sb("dtc", [P, 2, H8])
        dac = st.sb("dac", [P, 2, H8])
        xdt = st.sb("xdt", [P, H8, HD])
        xw = st.sb("xw", [P, H8, HD])
        ncum = st.sb("ncum", [P, H8])
        lw = st.sb("lw", [P, H8])
        last = st.sb("last", [P, H8])
        wst = st.sb("wst", [P, H8])
        ec = st.sb("ec", [P, H8])
        dec = st.sb("dec", [P, H8])
        cbm = st.sb("cbm", [P, GROUPS_D, P])
        ex = st.sb("ex", [P, H8, P])
        m = st.sb("m", [P, H8, P])
        carry = st.sb("carry", [P, 2, H8, HD])
        yt = st.sb("yt", [P, H8, HD])
        y = st.sb("y", [P, 2, INNER])
        CR = st.ps("cr", [P, H8, P])
        CC, CB, ST, OF, YD = (st.ps(n, [P, BANK]) for n in ("cc", "cb", "st", "of", "yd"))
        (dt_in, sp1, sp2, sp3, const_done, bc_in0, bc_in1, da_done, cum_done, ncum_done, lw_done, small_done, ex_done, xw_done,
         cb_done, cbm_done, m_done, of_done, st_done, carry_done, yt_done, yd_done, y_done, stored0, stored1, dve_step, act_step, pool_step) = (
             st.sem(n) for n in (
                 "dt_in sp1 sp2 sp3 const_done bc_in0 bc_in1 da_done cum_done ncum_done lw_done small_done ex_done xw_done "
                 "cb_done cbm_done m_done of_done st_done carry_done yt_done yd_done y_done stored0 stored1 dve_step act_step pool_step").split())
        bc_in, stored = (bc_in0, bc_in1), (stored0, stored1)

        def chunk(i, d):
            return i if d == 0 else i * -1 + (SCAN_TILES - 1)

        with nc.Block() as block:

            @block.sync
            def _(sp):
                rows = proj.rearrange("(t p) n -> p t n", p=P)
                for to, first, n in ((0, NTX, NTC), (NTC, 0, NTX), (NTC + NTX, NTX, NTC)):
                    sp.dma_start(dt[:, to:to + n, :], rows[:, first:first + n, DT0:DT0 + 2 * H8]).then_inc(dt_in, 16)
                for d in range(2):
                    sp.dma_start(alog[:, d * H8:(d + 1) * H8], row(a_logs[d], H8)).then_inc(dt_in, 16)
                    sp.dma_start(dtb[:, d * H8:(d + 1) * H8], row(dt_biases[d], H8)).then_inc(dt_in, 16)
                with sp.Fori(0, TURNS) as i:
                    for d in range(2):
                        sp.wait_ge(yd_done, i * 2 + (d + 1))
                        at = bass.ds(chunk(i, d) * P, P)
                        sp.dma_start(bc[:, d], by_channel[INNER:, at].rearrange("(c p) l -> p c l", p=P)).then_inc(bc_in[d], 16)
                        sp.dma_start(xb[:, d], by_token[at, 0:INNER + GROUPS_D * P]).then_inc(bc_in[d], 16)

            @block.gpsimd
            def _(pool):
                link = Link(pool, pool_step)
                link(nc.gpsimd.memset(tri[:], 1.0))
                link(nc.gpsimd.memset(carry[:], 0.0))
                link(nc.gpsimd.affine_select(out=tri[:, 0, :], in_=tri[:, 0, :], compare_op=ALU.is_ge, fill=0.0, base=0,
                                             pattern=[[1, P]], channel_multiplier=-1))
                link(nc.gpsimd.affine_select(out=tri[:, 1, :], in_=tri[:, 1, :], compare_op=ALU.is_ge, fill=0.0, base=0,
                                             pattern=[[-1, P]], channel_multiplier=1))
                pool.sem_inc(const_done, 1)

            @block.scalar
            def _(act):
                link = Link(act, act_step)
                act.wait_ge(sp1, 1)
                link(nc.scalar.activation(sp_a[:], sp_a[:], ACT.Exp, scale=-1.0))
                nc.scalar.activation(alog[:], alog[:], ACT.Exp).then_inc(sp2, 1)
                act.wait_ge(sp2, 1)
                nc.scalar.activation(sp_a[:], sp_a[:], ACT.Ln, bias=1.0).then_inc(sp2, 1)
                with act.Fori(0, TURNS) as i:
                    link.turn(i, 2)
                    for d in range(2):
                        act.wait_ge(yt_done, i * 2 + d)
                        act.wait_ge(carry_done, i * 2 + d)
                        act.wait_ge(lw_done, i * 2 + (d + 1))
                        nc.scalar.activation(ec[:], ncum[:], ACT.Exp, scale=-1.0)
                        nc.scalar.activation(dec[:], last[:], ACT.Exp)
                        nc.scalar.activation(wst[:], lw[:], ACT.Exp).then_inc(small_done, 1)
                        act.wait_ge(m_done, i * 2 + d)
                        for h in range(H8):
                            a = nc.scalar.activation(ex[:, h, :], CR[:, h, :], ACT.Abs, bias=ncum[:, h:h + 1])
                        link(a)
                        nc.scalar.activation(ex[:], ex[:], ACT.Exp, scale=-1.0).then_inc(ex_done, 1)
                        act.wait_ge(y_done, i * 2 + (d + 1))
                        at = act.snap(chunk(i, d) * P)
                        act.dma_start(y_out[d][bass.ds(at, P), :], y[:, d, :]).then_inc(stored[d], 16)
                link.over(TURNS)
                for d in range(2):
                    act.wait_ge(stored[d], 16 * TURNS)

            @block.vector
            def _(dve):
                link = Link(dve, dve_step)
                dve.wait_ge(dt_in, 16 * 7)
                per_tile = lambda v: v.unsqueeze(1).to_broadcast([P, SCAN_TILES, 2 * H8])
                link(nc.vector.tensor_tensor(dt[:], dt[:], per_tile(dtb[:]), ALU.add))
                link(nc.vector.tensor_scalar(sp_b[:], dt[:], -1.0, None, ALU.mult))
                nc.vector.tensor_tensor(sp_a[:], dt[:], sp_b[:], ALU.max).then_inc(sp1, 1)
                dve.wait_ge(sp1, 1)
                link(nc.vector.tensor_scalar(sp_b[:], dt[:], 0.0, None, ALU.max))
                dve.wait_ge(sp2, 2)
                link(nc.vector.tensor_tensor(dt[:], sp_b[:], sp_a[:], ALU.add))
                link(nc.vector.tensor_scalar(alog[:], alog[:], -1.0, None, ALU.mult))
                link(nc.vector.tensor_tensor(da[:], dt[:], per_tile(alog[:]), ALU.mult))
                dve.wait_ge(const_done, 1)
                per_head = lambda v, width=HD: v.unsqueeze(2).to_broadcast([P, H8, width])
                with dve.Fori(0, TURNS) as i:
                    link.turn(i, 2 * 4)
                    for d in range(2):
                        n = i * 2 + d
                        end = P - 1 if d == 0 else 0
                        here = dve.snap(chunk(i, d))
                        link(nc.vector.tensor_copy(dtc[:, d, :], dt[:, bass.ds(here, 1), d * H8:(d + 1) * H8].rearrange("p a h -> p (a h)")))
                        nc.vector.tensor_copy(dac[:, d, :], da[:, bass.ds(here, 1), d * H8:(d + 1) * H8].rearrange("p a h -> p (a h)")).then_inc(da_done, 1)
                        dve.wait_ge(bc_in[d], i * 32 + 32)
                        link(nc.vector.tensor_tensor(xdt[:], xb[:, d, 0:INNER].rearrange("p (h c) -> p h c", h=H8), per_head(dtc[:, d, :]), ALU.mult))
                        dve.wait_ge(cum_done, n + 1)
                        nc.vector.tensor_scalar(ncum[:], CC[:, 0:H8], -1.0, None, ALU.mult).then_inc(ncum_done, 1)
                        link(nc.vector.tensor_copy(last[:], CR[:, :, end]))
                        dve.wait_ge(ncum_done, n + 1)
                        nc.vector.tensor_tensor(lw[:], last[:], ncum[:], ALU.add).then_inc(lw_done, 1)
                        dve.wait_ge(small_done, n + 1)
                        nc.vector.tensor_tensor(xw[:], xdt[:], per_head(wst[:]), ALU.mult).then_inc(xw_done, 1)
                        dve.wait_ge(cb_done, n + 1)
                        nc.vector.tensor_tensor(cbm[:], CB[:, 0:GROUPS_D * P].rearrange("p (g l) -> p g l", g=GROUPS_D),
                                                tri[:, d, :].unsqueeze(1).to_broadcast([P, GROUPS_D, P]), ALU.mult).then_inc(cbm_done, 1)
                        dve.wait_ge(cbm_done, n + 1)
                        dve.wait_ge(ex_done, n + 1)
                        each = H8 // GROUPS_D
                        for g in range(GROUPS_D):
                            mul = nc.vector.tensor_tensor(m[:, g * each:(g + 1) * each, :], ex[:, g * each:(g + 1) * each, :],
                                                          cbm[:, g, :].unsqueeze(1).to_broadcast([P, each, P]), ALU.mult)
                        mul.then_inc(m_done, 1)
                        dve.wait_ge(of_done, n + 1)
                        nc.vector.tensor_tensor(yt[:], OF[:].rearrange("p (h c) -> p h c", h=H8), per_head(ec[:]), ALU.mult).then_inc(yt_done, 1)
                        link(nc.vector.tensor_tensor(carry[:, d], carry[:, d], per_head(dec[:]), ALU.mult))
                        dve.wait_ge(st_done, n + 1)
                        nc.vector.tensor_tensor(carry[:, d], ST[:].rearrange("p (h c) -> p h c", h=H8), carry[:, d], ALU.add).then_inc(carry_done, 1)
                        dve.wait_ge(yd_done, n + 3)
                        dve.wait_ge(yt_done, n + 1)
                        dve.wait_ge(stored[d], i * 16)
                        nc.vector.tensor_tensor(y[:, d, :], YD[:], yt[:].rearrange("p h c -> p (h c)"), ALU.add).then_inc(y_done, 1)
                link.over(TURNS)

            @block.tensor
            def _(pe):
                pe.sem_inc(yd_done, 2)
                pe.wait_ge(const_done, 1)
                with pe.Fori(0, TURNS) as i:
                    for d in range(2):
                        n = i * 2 + d
                        pe.wait_ge(da_done, n + 1)
                        pe.wait_ge(ex_done, n)
                        for h in range(H8):
                            nc.tensor.matmul(CR[:, h, :], dac[:, d, h:h + 1].to_broadcast([P, P]), tri[:, d, :], start=True, stop=True)
                        nc.tensor.matmul(CC[:, 0:H8], tri[:, d, :], dac[:, d, :], start=True, stop=True).then_inc(cum_done, 1)
                        pe.wait_ge(bc_in[d], i * 32 + 32)
                        pe.wait_ge(cbm_done, n)
                        for g in range(GROUPS_D):
                            mm = nc.tensor.matmul(CB[:, g * P:(g + 1) * P], bc[:, d, g, :], bc[:, d, GROUPS_D + g, :], start=True, stop=True)
                        mm.then_inc(cb_done, 1)
                        half = INNER // GROUPS_D
                        state = carry[:, d].rearrange("p h c -> p (h c)")
                        pe.wait_ge(yt_done, n)
                        pe.wait_ge(carry_done, n)
                        for g in range(GROUPS_D):
                            mm = nc.tensor.matmul(OF[:, g * half:(g + 1) * half], bc[:, d, GROUPS_D + g, :], state[:, g * half:(g + 1) * half],
                                                  start=True, stop=True)
                        mm.then_inc(of_done, 1)
                        pe.wait_ge(xw_done, n + 1)
                        for g in range(GROUPS_D):
                            mm = nc.tensor.matmul(ST[:, g * half:(g + 1) * half], xb[:, d, INNER + g * P:INNER + (g + 1) * P],
                                                  xw[:].rearrange("p h c -> p (h c)")[:, g * half:(g + 1) * half], start=True, stop=True)
                        mm.then_inc(st_done, 1)
                        pe.wait_ge(m_done, n + 1)
                        pe.wait_ge(y_done, n)
                        for h in range(H8):
                            mm = nc.tensor.matmul(YD[:, h * HD:(h + 1) * HD], m[:, h, :], xdt[:, h, :], start=True, stop=True)
                        mm.then_inc(yd_done, 1)


def scan_out(nc, K, proj, by_token, y_in, d_skip, gnorm_g, out):
    GW = INNER // GROUPS_D
    with Stage(nc, "scan_out") as st:
        yf = st.sb("yf", [P, INNER])
        yb = st.sb("yb", [P, INNER])
        xs = st.sb("xs", [P, INNER])
        z = st.sb("z", [P, INNER])
        o = st.sb("o", [P, INNER])
        sq = st.sb("sq", [P, GW])
        ms = st.sb("ms", [P, GROUPS_D])
        skip = st.sb("skip", [P, HEADS_D])
        gn = st.sb("gn", [P, INNER])
        const_in, in_done, sum_done, sil_done, g_done, ms_done, rs_done, o_done, stored, dve_step, act_step, pool_step = (
            st.sem(n) for n in "const_in in_done sum_done sil_done g_done ms_done rs_done o_done stored dve_step act_step pool_step".split())

        with nc.Block() as block:

            @block.sync
            def _(sp):
                sp.dma_start(skip[:], row(d_skip, HEADS_D)).then_inc(const_in, 16)
                sp.dma_start(gn[:], row(gnorm_g, INNER)).then_inc(const_in, 16)
                with sp.Fori(0, NTX) as t:
                    sp.wait_ge(o_done, t)
                    at, scan_at = bass.ds(t * P, P), bass.ds(t * P + CTX, P)
                    sp.dma_start(yf[:], y_in[0][scan_at, :]).then_inc(in_done, 16)
                    sp.dma_start(yb[:], y_in[1][scan_at, :]).then_inc(in_done, 16)
                    sp.dma_start(xs[:], by_token[scan_at, 0:INNER]).then_inc(in_done, 16)
                    sp.dma_start(z[:], proj[at, Z0:Z0 + INNER]).then_inc(in_done, 16)

            @block.gpsimd
            def _(pool):
                link = Link(pool, pool_step)
                with pool.Fori(0, NTX) as t:
                    link.turn(t, 1)
                    pool.wait_ge(in_done, t * 64 + 64)
                    nc.gpsimd.tensor_tensor(yf[:], yf[:], yb[:], ALU.add).then_inc(sum_done, 1)
                    pool.wait_ge(ms_done, t * 2 + 2)
                    link(nc.gpsimd.tensor_tensor(ms[:], ms[:], K.eps[:, 0:GROUPS_D], ALU.add))
                    nc.gpsimd.tensor_tensor(ms[:], ms[:], K.neg_half[:, 0:GROUPS_D], ALU.pow).then_inc(rs_done, 1)
                link.over(NTX)

            @block.scalar
            def _(act):
                link = Link(act, act_step)
                with act.Fori(0, NTX) as t:
                    act.wait_ge(in_done, t * 64 + 64)
                    nc.scalar.activation(z[:], z[:], ACT.Silu).then_inc(sil_done, 1)
                    act.wait_ge(g_done, t + 1)
                    for g in range(GROUPS_D):
                        nc.scalar.activation(sq[:], yf[:, g * GW:(g + 1) * GW], ACT.Square, scale=GW ** -0.5,
                                             accum_out=ms[:, g:g + 1]).then_inc(ms_done, 1)
                        act.wait_ge(ms_done, t * 2 + (g + 1))
                    act.wait_ge(o_done, t + 1)
                    at = act.snap(t * P)
                    act.dma_start(out[bass.ds(at, P), INNER:2 * INNER], o[:]).then_inc(stored, 16)
                act.wait_ge(stored, 16 * NTX)

            @block.vector
            def _(dve):
                link = Link(dve, dve_step)
                dve.wait_ge(const_in, 32)
                with dve.Fori(0, NTX) as t:
                    link.turn(t, 2)
                    dve.wait_ge(in_done, t * 64 + 64)
                    heads = lambda v: v[:].rearrange("p (h c) -> p h c", h=HEADS_D)
                    link(nc.vector.tensor_tensor(heads(xs), heads(xs), skip[:].unsqueeze(2).to_broadcast([P, HEADS_D, HD]), ALU.mult))
                    dve.wait_ge(sum_done, t + 1)
                    link(nc.vector.tensor_tensor(yf[:], yf[:], xs[:], ALU.add))
                    dve.wait_ge(sil_done, t + 1)
                    nc.vector.tensor_tensor(yf[:], yf[:], z[:], ALU.mult).then_inc(g_done, 1)
                    dve.wait_ge(rs_done, t + 1)
                    dve.wait_ge(stored, t * 16)
                    for g in range(GROUPS_D):
                        part = slice(g * GW, (g + 1) * GW)
                        v = nc.vector.scalar_tensor_tensor(o[:, part], yf[:, part], ms[:, g:g + 1], gn[:, part], ALU.mult, ALU.mult)
                    v.then_inc(o_done, 1)
                link.over(NTX)


def trunk(nc, t, out):

    def dram(name, shape, dt=F32):
        return nc.dram_tensor(name, shape, dt, kind="Internal").ap()

    res = dram("res", (ROWS, D))
    normed = dram("normed", (ROWS, D))
    mixed = dram("mixed", (ROWS, D))
    moe = dram("moe", (ROWS, D))
    affinity = dram("affinity", (E, ROWS))
    mods = [dram(f"mod{n}", (2, 6 * D)) for n in range(2)]
    projs = [dram(f"proj{n}", (ROWS, t[f"l{n}_w_in"].shape[1])) for n in range(2)]
    skewed, lines = dram("skewed", (64 * (8 * 15 * 96 + 1),)), dram("lines", (64, 8 * 15 * 64))
    by_channel, by_token = dram("by_channel", (2 * INNER, SCAN_ROWS)), dram("by_token", (SCAN_ROWS, 2 * INNER))
    scanned = [dram(f"scanned{d}", (SCAN_ROWS, INNER)) for d in range(2)]
    choice = (dram("index", (E + 1, CAPX), I32), dram("weight", (E, CAPX)),
              dram("index_c", (E + 1, CAPC), I32), dram("weight_c", (E, CAPC)))
    rope = (t["rope_cos"], t["rope_sin"])

    with ExitStack() as stack, nc.allow_non_contiguous_dma(reason="vectors are spread over the partitions, and weights read in column blocks"):
        K = Constants(nc, stack)
        modulation(nc, t["c"], t["c_ctx"], t["x"], t["ctx"], [(t[f"l{n}_w_mod"], t[f"l{n}_b_mod"], mods[n]) for n in range(2)], res)
        for n in range(2):
            layer = {name[3:]: ap for name, ap in t.items() if name.startswith(f"l{n}_")}
            with_ctx = n == 0
            tiles = NT if with_ctx else NTX
            project(nc, f"proj{n}", K, res, mods[n], layer["g_pre_mix"], layer["w_in"], projs[n])
            if n == 0:
                differential_attention(nc, K, projs[n], *rope, [layer[f"lam_{v}"] for v in ("q1", "k1", "q2", "k2")],
                                       layer["subln_g"], n, mixed)
                local_attention(nc, K, "near", projs[n], mixed, rpb=layer["rpb"], scratch=(skewed, lines))
            else:
                local_attention(nc, K, "band", projs[n], mixed, rope=rope, sinks=layer["sinks"])
                convolve(nc, K, projs[n], layer["conv_w"], layer["conv_b"], by_channel, by_token)
                scan(nc, K, projs[n], by_channel, by_token, (layer["a_log_f"], layer["a_log_b"]),
                     (layer["dt_bias_f"], layer["dt_bias_b"]), scanned)
                scan_out(nc, K, projs[n], by_token, scanned, layer["d_skip"], layer["gnorm_g"], mixed)
            mix_out(nc, f"mix{n}", K, tiles, mixed, layer["w_out"], mods[n], layer["g_post_mix"], layer["g_pre_ffn"],
                    layer["w_router"], res, normed, affinity)
            choose(nc, f"choose{n}", with_ctx, affinity, *choice)
            experts(nc, f"experts{n}", K, with_ctx, normed, mods[n], layer["g_pre_ffn"], *choice,
                    layer["w_gate"], layer["w_up"], layer["w_down"], moe)
            finish(nc, f"finish{n}", K, tiles, moe, mods[n], layer["g_post_ffn"], res, res if with_ctx else out[0])


_COMMON = ["w_mod", "b_mod", "g_pre_mix", "g_post_mix", "g_pre_ffn", "g_post_ffn", "w_in", "w_out",
           "w_router", "w_gate", "w_up", "w_down"]
_INS = (["x", "c", "ctx", "c_ctx"] + [f"l{n}_{name}" for n in range(2) for name in _COMMON]
        + [f"l0_{name}" for name in ("lam_q1", "lam_k1", "lam_q2", "lam_k2", "subln_g", "rpb")]
        + [f"l1_{name}" for name in ("sinks", "conv_w", "conv_b", "a_log_f", "a_log_b", "dt_bias_f", "dt_bias_b", "d_skip", "gnorm_g")])


def rope_tables():
    import numpy as np

    token = np.arange(SEQ)
    freq = np.float32(10000.0) ** (-np.arange(HD // 4, dtype=np.float32) / np.float32(HD // 4))
    angle = np.concatenate([(token // 64).astype(np.float32)[:, None] * freq, (token % 64).astype(np.float32)[:, None] * freq], axis=-1)
    return np.tile(np.cos(angle), (1, 2)), np.tile(np.sin(angle), (1, 2))


def kernel(**inputs):
    import numpy as np
    import concourse.bacc as bacc
    from concourse.bass_utils import run_bass_kernel_spmd

    nc = bacc.Bacc("TRN2", target_bir_lowering=False, num_devices=1)
    arrays = {f"in_{name}": np.ascontiguousarray(inputs[name]) for name in _INS}
    arrays["in_rope_cos"], arrays["in_rope_sin"] = rope_tables()
    args = {name[3:]: nc.dram_tensor(name, a.shape, mybir.dt.from_np(a.dtype), kind="ExternalInput").ap()
            for name, a in arrays.items()}
    out = nc.dram_tensor("out_dram", (1, SEQ, D), F32, kind="ExternalOutput").ap()
    trunk(nc, args, out)
    r = run_bass_kernel_spmd(nc, [arrays], core_ids=[0])
    return r.results[0]["out_dram"]
```
